# Optimizing a Trainium2 kernel written in Bass

```python
import math
import jax, jax.numpy as jnp
from jax import lax
import numpy as np

D_MODEL = 1024
BATCH = 1
SEQ = 512
DEPTH = 2

MEM_LEN = 256
D_POOL = D_MODEL // 2
POOL_WINDOWS = (2, 4, 8, 16)
N_POOL_GROUPS = len(POOL_WINDOWS)
POOL_GROUP_DIM = D_POOL // N_POOL_GROUPS
D_SG = D_MODEL // 2
N_SG_HEADS = 4
SG_HEAD_DIM = D_SG // N_SG_HEADS
CHUNK = 128
D_CONV = D_MODEL
CONV_WIDTH = 3
N_XHEADS = 4
XHEAD_DIM = D_MODEL // N_XHEADS
N_GROUPS = 4
EXPERTS_PER_GROUP = 8
N_EXPERTS = N_GROUPS * EXPERTS_PER_GROUP
TOP_K_INNER = 2
D_EXPERT = 512
DISPATCH_BLOCK = 128
N_EVEN = (DEPTH + 1) // 2
N_ODD = DEPTH // 2
ALPHA = (2.0 * DEPTH) ** 0.25
BETA = (8.0 * DEPTH) ** -0.25
LN_EPS = 1e-5

kernel_name = "hybrid_pool_sgate_shortconv_hmoe_deepnorm"

def layer_norm(x, g, b):
    xf = x.astype(jnp.float32)
    mu = jnp.mean(xf, axis=-1, keepdims=True)
    var = jnp.mean(jnp.square(xf - mu), axis=-1, keepdims=True)
    y = (xf - mu) * lax.rsqrt(var + LN_EPS)
    return (y * g.astype(jnp.float32) + b.astype(jnp.float32)).astype(x.dtype)

def pool_mixer(a, w_pool, pool_scale):
    B, S, _ = a.shape
    a4 = a.astype(jnp.float32).reshape(B, S, N_POOL_GROUPS, POOL_GROUP_DIM)
    cs = jnp.cumsum(a4, axis=1)
    pos = jnp.arange(1, S + 1, dtype=jnp.float32)
    diffs = []
    for g, w in enumerate(POOL_WINDOWS):
        cs_g = cs[:, :, g]
        lagged = jnp.pad(cs_g, ((0, 0), (w, 0), (0, 0)))[:, :S]
        cnt = jnp.minimum(pos, float(w))[None, :, None]
        diffs.append((cs_g - lagged) / cnt - a4[:, :, g])
    d = jnp.stack(diffs, axis=2)
    y = jnp.einsum('bsgc,gcd->bsgd', d, w_pool.astype(jnp.float32))
    y = y.reshape(B, S, D_POOL) * pool_scale.astype(jnp.float32)
    return y.astype(a.dtype)

def spatial_gating(z, ln_v_g, ln_v_b, w_spatial, b_spatial):
    B, S, _ = z.shape
    u, v = z[..., :D_SG], z[..., D_SG:]
    v = layer_norm(v, ln_v_g, ln_v_b)
    vc = v.reshape(B, S // CHUNK, CHUNK, N_SG_HEADS, SG_HEAD_DIM)
    mask = jnp.tril(jnp.ones((CHUNK, CHUNK), dtype=w_spatial.dtype))
    ws = w_spatial * mask[None]
    sv = jnp.einsum('hij,bnjhc->bnihc', ws, vc) + b_spatial.T[:, :, None]
    return u * sv.reshape(B, S, D_SG)

def even_mixer(x, w_in, w_pool, pool_scale, ln_v_g, ln_v_b, w_spatial, b_spatial, w_out):
    h = x @ w_in
    a_out = pool_mixer(h[..., :D_POOL], w_pool, pool_scale)
    b_out = spatial_gating(jax.nn.gelu(h[..., D_POOL:]), ln_v_g, ln_v_b, w_spatial, b_spatial)
    return jnp.concatenate([a_out, b_out], axis=-1) @ w_out

def odd_mixer(x, w_in, conv_w, conv_b, w_out):
    S = x.shape[1]
    h = x @ w_in
    bg, cg, z = h[..., :D_CONV], h[..., D_CONV:2 * D_CONV], h[..., 2 * D_CONV:]
    zc = cg * z
    zp = jnp.pad(zc, ((0, 0), (CONV_WIDTH - 1, 0), (0, 0)))
    conv = conv_b + zp[:, 0:S] * conv_w[:, 0] + zp[:, 1:S + 1] * conv_w[:, 1] + zp[:, 2:S + 2] * conv_w[:, 2]
    return (bg * conv) @ w_out

def memory_cross_attn(x, mem, wq, wk, wv, wo):
    B, S, D = x.shape
    M = mem.shape[1]
    q = (x @ wq).reshape(B, S, N_XHEADS, XHEAD_DIM)
    k = (mem @ wk).reshape(B, M, N_XHEADS, XHEAD_DIM)
    v = (mem @ wv).reshape(B, M, N_XHEADS, XHEAD_DIM)
    s = jnp.einsum('bshd,bmhd->bhsm', q, k).astype(jnp.float32) / math.sqrt(XHEAD_DIM)
    p = jax.nn.softmax(s, axis=-1).astype(v.dtype)
    o = jnp.einsum('bhsm,bmhd->bshd', p, v).reshape(B, S, D)
    return o @ wo

def expert_dispatch(xf, expert_ids, gates, w1, w3, w2):
    N, D = xf.shape
    A = N * TOP_K_INNER
    e_flat = expert_ids.reshape(-1)
    g_flat = gates.reshape(-1)
    tok = jnp.arange(A, dtype=jnp.int32) // TOP_K_INNER
    order = jnp.argsort(e_flat)
    se, stok, sg = e_flat[order], tok[order], g_flat[order]
    counts = jnp.zeros((N_EXPERTS,), jnp.int32).at[e_flat].add(1)
    start = jnp.cumsum(counts) - counts
    pcounts = (counts + DISPATCH_BLOCK - 1) // DISPATCH_BLOCK * DISPATCH_BLOCK
    pend = jnp.cumsum(pcounts)
    pstart = pend - pcounts
    dest = pstart[se] + (jnp.arange(A, dtype=jnp.int32) - start[se])
    n_blocks = (A + N_EXPERTS * (DISPATCH_BLOCK - 1) + DISPATCH_BLOCK - 1) // DISPATCH_BLOCK
    P = n_blocks * DISPATCH_BLOCK
    buf_tok = jnp.full((P,), N, jnp.int32).at[dest].set(stok)
    buf_gate = jnp.zeros((P,), gates.dtype).at[dest].set(sg)
    block_e = jnp.minimum(
        jnp.searchsorted(pend, jnp.arange(n_blocks, dtype=jnp.int32) * DISPATCH_BLOCK, side='right'),
        N_EXPERTS - 1)
    xpad = jnp.concatenate([xf, jnp.zeros((1, D), xf.dtype)], axis=0)
    xb = xpad[buf_tok].reshape(n_blocks, DISPATCH_BLOCK, D)

    def expert_block(args):
        xblk, e = args
        hid = jax.nn.silu(xblk @ w1[e]) * (xblk @ w3[e])
        return hid @ w2[e]

    yb = lax.map(expert_block, (xb, block_e)).reshape(P, D) * buf_gate[:, None]
    return jnp.zeros((N + 1, D), yb.dtype).at[buf_tok].add(yb)[:N]

def hierarchical_moe(x, wr_g, br_g, wr_e, br_e, w1, w3, w2):
    B, S, D = x.shape
    xf = x.reshape(B * S, D)
    x32 = xf.astype(jnp.float32)
    logits_g = x32 @ wr_g.astype(jnp.float32) + br_g.astype(jnp.float32)
    p_g = jax.nn.softmax(logits_g, axis=-1)
    g_sel = jnp.argmax(logits_g, axis=-1).astype(jnp.int32)
    gate_g = jnp.take_along_axis(p_g, g_sel[:, None], axis=1)[:, 0]
    logits_all = jnp.einsum('nd,gde->nge', x32, wr_e.astype(jnp.float32)) + br_e.astype(jnp.float32)
    logits_e = jnp.take_along_axis(logits_all, g_sel[:, None, None], axis=1)[:, 0]
    top_v, top_i = lax.top_k(logits_e, TOP_K_INNER)
    w_inner = jax.nn.softmax(top_v, axis=-1)
    expert_ids = g_sel[:, None] * EXPERTS_PER_GROUP + top_i.astype(jnp.int32)
    gates = (gate_g[:, None] * w_inner).astype(x.dtype)
    y = expert_dispatch(xf, expert_ids, gates, w1, w3, w2)
    return y.reshape(B, S, D)

def setup_inputs(seed: int = 0) -> dict:
    key = jax.random.key(seed)
    ks = iter(jax.random.split(key, 40))
    f32 = jnp.float32
    D = D_MODEL

    def nrm(shape, scale):
        return jax.random.normal(next(ks), shape, f32) * scale

    d_in_even = D_POOL + 2 * D_SG
    return {
        "x": nrm((BATCH, SEQ, D), 1.0),
        "mem": nrm((BATCH, MEM_LEN, D), 1.0),
        "w_in_even": nrm((N_EVEN, D, d_in_even), D ** -0.5),
        "w_pool": nrm((N_EVEN, N_POOL_GROUPS, POOL_GROUP_DIM, POOL_GROUP_DIM), POOL_GROUP_DIM ** -0.5),
        "pool_scale": 1.0 + nrm((N_EVEN, D_POOL), 0.1),
        "ln_v_g": 1.0 + nrm((N_EVEN, D_SG), 0.02),
        "ln_v_b": nrm((N_EVEN, D_SG), 0.02),
        "w_spatial": nrm((N_EVEN, N_SG_HEADS, CHUNK, CHUNK), CHUNK ** -0.5),
        "b_spatial": 1.0 + nrm((N_EVEN, N_SG_HEADS, CHUNK), 0.1),
        "w_out_even": nrm((N_EVEN, D_POOL + D_SG, D), (D_POOL + D_SG) ** -0.5 * BETA),
        "w_in_odd": nrm((N_ODD, D, 3 * D_CONV), D ** -0.5),
        "conv_w": nrm((N_ODD, D_CONV, CONV_WIDTH), CONV_WIDTH ** -0.5),
        "conv_b": nrm((N_ODD, D_CONV), 0.02),
        "w_out_odd": nrm((N_ODD, D_CONV, D), D_CONV ** -0.5 * BETA),
        "wq_x": nrm((DEPTH, D, D), D ** -0.5),
        "wk_x": nrm((DEPTH, D, D), D ** -0.5),
        "wv_x": nrm((DEPTH, D, D), D ** -0.5 * BETA),
        "wo_x": nrm((DEPTH, D, D), D ** -0.5 * BETA),
        "ln_g": 1.0 + nrm((DEPTH, 3, D), 0.02),
        "ln_b": nrm((DEPTH, 3, D), 0.02),
        "wr_group": nrm((DEPTH, D, N_GROUPS), D ** -0.5),
        "br_group": nrm((DEPTH, N_GROUPS), 0.01),
        "wr_expert": nrm((DEPTH, N_GROUPS, D, EXPERTS_PER_GROUP), D ** -0.5),
        "br_expert": nrm((DEPTH, N_GROUPS, EXPERTS_PER_GROUP), 0.01),
        "w1": nrm((DEPTH, N_EXPERTS, D, D_EXPERT), D ** -0.5),
        "w3": nrm((DEPTH, N_EXPERTS, D, D_EXPERT), D ** -0.5),
        "w2": nrm((DEPTH, N_EXPERTS, D_EXPERT, D), D_EXPERT ** -0.5 * BETA),
    }

def reference(x, mem, w_in_even, w_pool, pool_scale, ln_v_g, ln_v_b, w_spatial, b_spatial,
              w_out_even, w_in_odd, conv_w, conv_b, w_out_odd, wq_x, wk_x, wv_x, wo_x,
              ln_g, ln_b, wr_group, br_group, wr_expert, br_expert, w1, w3, w2):
    for l in range(DEPTH):
        i = l // 2
        if l % 2 == 0:
            mix = even_mixer(x, w_in_even[i], w_pool[i], pool_scale[i], ln_v_g[i], ln_v_b[i],
                             w_spatial[i], b_spatial[i], w_out_even[i])
        else:
            mix = odd_mixer(x, w_in_odd[i], conv_w[i], conv_b[i], w_out_odd[i])
        x = layer_norm(ALPHA * x + mix, ln_g[l, 0], ln_b[l, 0])
        xa = memory_cross_attn(x, mem, wq_x[l], wk_x[l], wv_x[l], wo_x[l])
        x = layer_norm(ALPHA * x + xa, ln_g[l, 1], ln_b[l, 1])
        ff = hierarchical_moe(x, wr_group[l], br_group[l], wr_expert[l], br_expert[l],
                              w1[l], w3[l], w2[l])
        x = layer_norm(ALPHA * x + ff, ln_g[l, 2], ln_b[l, 2])
    return x


_drawn_inputs = setup_inputs


def setup_inputs(seed=0):
    import zlib

    import numpy as np

    out = dict(_drawn_inputs(seed))
    spreads = {}
    factors = {'ln_v_g': 24.374,
     'ln_v_b': 22.972,
     'conv_b': 5.206,
     'br_group': 47.615,
     'br_expert': 7.54,
     'b_spatial': 3.417}
    for name, (base, spread) in spreads.items():
        noise = np.random.default_rng([zlib.crc32(name.encode()), seed]).standard_normal(out[name].shape)
        drawn = base * np.exp(spread * noise) if base else spread * noise
        out[name] = __import__('jax').numpy.asarray(drawn.astype(out[name].dtype))
    for name, factor in factors.items():
        out[name] = (out[name] * factor).astype(out[name].dtype)
    return out
```

```python
from contextlib import ExitStack

import concourse.bass as bass
from concourse import mybir

F32, F32R, I32 = mybir.dt.float32, mybir.dt.float32r, mybir.dt.int32
ALU, ACT, AX = mybir.AluOpType, mybir.ActivationFunctionType, mybir.AxisListType

P = 128
D = 1024
KD = D // P
S = 512
TT = S // P
MEM = 256
MT = MEM // P
HALF = 512
SG_HEADS = 4
HEADS, HEAD_DIM = 4, 256
WINDOWS = (2, 4, 8, 16)
PAD = max(WINDOWS)
GROUPS, PER_GROUP = 4, 8
EXPERTS = GROUPS * PER_GROUP
HID = 512
NROUTE = GROUPS + EXPERTS
DEPTH = 2
ALPHA = (2.0 * DEPTH) ** 0.25
LN_EPS = 1e-5
SCALE = HEAD_DIM ** -0.5

SLOTS = 64
PAIRS = EXPERTS // 2
MORE_BLOCKS = 2 * S // SLOTS
MORE_PAIRS = MORE_BLOCKS // 2
BLOCKS = EXPERTS + MORE_BLOCKS + 4
INVALID = 1 << 20
BIG = 1e30

RING = 6
RAW = 2
SPLIT_HALVES = 2
BANKS = 8
PAIR_TILES = 6
XG0, XG1, HA, HB, TA, YA, TB, YB = range(8)
TILE_LAST = (HA, HA, HB, HB, YA, YB)
TILE_SLOT = (2, 3, 4, 5, 1, 0)
ROWS_ORDER = ((0, 0), (1, 0), (0, 1), (1, 1), (2, 0), (3, 0), (2, 1), (3, 1))


def schedule():
    jobs, stream = {}, []
    count = [0]

    def job(*name):
        jobs[name] = count[0]
        count[0] += 1
        return jobs[name]

    def tile(kind, what, l, c, *last):
        stream.append((kind, (what, l, c), jobs.get(last)))

    def proj_rows(l, what):
        for t, c in ROWS_ORDER:
            job(what, l, t, c)
        for c in range(2):
            tile("split", what, l, c, what, l, TT - 1, c)

    def k_tile(l, c):
        for j in range(2):
            job("k", l, c, j)
        tile("whole", "k", l, c, "k", l, c, 1)

    def v_tile(l, c):
        for m in range(MT):
            job("v", l, c, m)
        tile("whole", "v", l, c, "v", l, c, MT - 1)

    def xt_jobs(site, ts):
        for t in ts:
            for g in range(2):
                job("xt", site, t, g)

    def first_pair(l, js):
        for j in js:
            tile("moe", "moe", l, j)

    xt_jobs(0, range(TT))
    for l in range(DEPTH):
        if l == 0:
            for what in ("gate_v", "pool_a", "gate_u"):
                for m in range(4):
                    job(what, m)
                tile("split", what, l, 0, what, 3)
            job("wst")
            for g in range(4):
                job("pool_y", g)
            for h in range(SG_HEADS):
                job("spatial", h)
            for m in range(MT):
                for g in range(2):
                    job("memt", m, g)
        else:
            for c in range(2):
                for what in ("cg", "z", "bg"):
                    for m in range(4):
                        job(what, c, m)
                    tile("split", what, l, c, what, c, 3)
        proj_rows(l, "mix")
        if l == 0:
            for c in range(2):
                k_tile(l, c)
            for c in range(2):
                v_tile(l, c)
        xt_jobs(3 * l + 1, range(TT))
        for c in range(2):
            for m in range(4):
                job("q", l, c, m)
            tile("split", "q", l, c, "q", l, c, 3)
        job("s", l, 0)
        job("s", l, 1)
        for j in range(8):
            if j + 2 < 8:
                job("s", l, j + 2)
            job("pt", l, j)
        for n in range(8):
            job("o", l, n)
        proj_rows(l, "wo")
        xt_jobs(3 * l + 2, range(TT - 1))
        if l == 0:
            k_tile(1, 0)
        xt_jobs(3 * l + 2, [TT - 1])
        job("route", l)
        if l == 0:
            k_tile(1, 1)
            first_pair(l, (0, 1))
        job("rank", l)
        if l == 0:
            v_tile(1, 0)
            first_pair(l, (2, 3))
        job("table", l)
        if l == 0:
            v_tile(1, 1)
            first_pair(l, (4, 5))
        else:
            first_pair(l, range(PAIR_TILES))
        jobs["moe", l] = count[0]
        tile("pairs", "moe", l, None)
        count[0] += BANKS * PAIRS
        if l + 1 < DEPTH:
            xt_jobs(3 * l + 3, range(TT))
    return jobs, stream


def place_tiles(jobs, stream):
    uses, release = [0] * RING, [None] * RING
    tile_slots, splits, moe_uses = {}, {}, {}
    raws = 0
    for kind, name, last in stream:
        if kind in ("split", "whole"):
            slot = raws % RAW
            raws += 1
            free = release[slot]
            if kind == "split":
                number = len(splits)
                splits[name] = (number, last)
                release[slot] = ("split", number)
                for n in range(2):
                    release[RAW + 2 * (number % 2) + n] = ("filled", last)
            else:
                release[slot] = ("filled", last)
        elif kind == "moe":
            l, j = name[1:]
            slot = TILE_SLOT[j]
            moe_uses.setdefault(l, {})[slot] = uses[slot]
            free = release[slot]
        else:
            l = name[1]
            for j, slot in enumerate(TILE_SLOT):
                uses[slot] += PAIRS - 1
                release[slot] = ("filled", jobs["moe", l] + BANKS * (PAIRS - 1) + TILE_LAST[j])
            continue
        uses[slot] += 1
        tile_slots[name] = (slot, uses[slot], free)
    return tile_slots, splits, moe_uses


def count_highs():
    done, total = {}, 0
    for l in range(DEPTH):
        for step, n in ((("xt", 3 * l), 2 * TT), (("mix", l), TT if l else KD), (("xt", 3 * l + 1), 2 * TT), (("o", l), KD)):
            total += n
            done[step] = total
    return done


class Signals:

    def __init__(self, landed, filled, drained, gathered, silu, index_ready, stored, pool_step,
                 job0, slot_uses, runs, pair0, pairs):
        self.landed, self.filled, self.drained = landed, filled, drained
        self.gathered, self.silu, self.index_ready, self.stored = gathered, silu, index_ready, stored
        self.pool_step = pool_step
        self.job0, self.slot_uses, self.pair0, self.pairs = job0, slot_uses, pair0, pairs
        self.rounds = pairs // 2
        self.gathered0 = (self.rounds + 1) * runs
        self.silu0 = 2 * pairs * runs
        self.index0 = ((self.rounds + 1) * runs, self.rounds * runs)
        self.stored0 = self.rounds * runs
        self.step0 = (pairs + 2) * runs

    def bank(self, j):
        return (self.job0 + j) % BANKS

    def wait_filled(self, eng, j, p, before=0):
        eng.wait_ge(self.filled[self.bank(j)], (self.job0 + j) // BANKS + 1 - before + p)

    def wait_drained(self, eng, j, p, before=0):
        eng.wait_ge(self.drained[self.bank(j)], (self.job0 + j) // BANKS + 1 - before + p)


def trunk(nc, x, mem, w_in_even, w_pool, pool_scale, ln_v_g, ln_v_b, w_spatial, b_spatial,
          w_out_even, w_in_odd, conv_w, conv_b, w_out_odd, wq_x, wk_x, wv_x, wo_x,
          ln_g, ln_b, wr_group, br_group, wr_expert, br_expert, w1, w3, w2, out):
    jobs, stream = schedule()
    tile_slots, splits, moe_uses = place_tiles(jobs, stream)
    highs_done = count_highs()

    with ExitStack() as ctx:
        def sb(name, shape, dt=F32):
            return ctx.enter_context(nc.sbuf_tensor(name, shape, dt))

        def sem(name):
            return ctx.enter_context(nc.semaphore(name))

        def parts(name, at_, chunks, width):
            return nc.alloc_sbuf_tensor_at(name, [P, chunks, width], F32R, offset=at_)

        def next_at():
            return (nc.sbuf_base + 31) // 32 * 32

        ring_at = next_at()
        ring = sb("ring", [P, RING, KD * HALF])
        xs = sb("xs", [P, TT, D])
        area_x_at = next_at()
        area_x = sb("area_x", [P, 4096])
        area_a_at = next_at()
        area_a = sb("area_a", [P, 4096])
        area_b_at = next_at()
        area_b = sb("area_b", [P, 4160])
        slot_bytes = 4 * KD * HALF
        w_hi = [parts(f"w_hi{n}", ring_at + (RAW + 2 * n) * slot_bytes, KD, HALF) for n in range(2)]
        w_lo = [parts(f"w_lo{n}", ring_at + (RAW + 2 * n + 1) * slot_bytes, KD, HALF) for n in range(2)]
        x_hi, x_lo = parts("x_hi", area_x_at, KD, S), parts("x_lo", area_a_at, KD, S)
        o_hi, o_lo = parts("o_hi", area_a_at, KD, S), parts("o_lo", area_b_at, KD, S)
        area_kv = sb("area_kv", [P, 4096])
        area_e = sb("area_e", [P, 2560])
        work = sb("work", [P, 2, D])
        gb = sb("gb", [P, 2, D])
        ident = sb("ident", [P, P])
        ones = sb("ones", [P, P])
        before = sb("before", [P, P])
        wr = sb("wr", [P, KD, NROUTE])
        br = sb("br", [P, NROUTE])
        stats = sb("stats", [P, 12])
        mean_var = [sb(f"mean_var{n}", [P, 2]) for n in range(2)]
        var_eps = [sb(f"var_eps{n}", [P, 1]) for n in range(2)]
        rstd = [sb(f"rstd{n}", [P, 1]) for n in range(2)]
        minus_half = sb("minus_half", [P, 1])
        pscale = sb("pscale", [P, 4])
        inv_count = sb("inv_count", [P, PAD])
        convw = sb("convw", [P, KD, 3])
        convb = sb("convb", [P, KD])
        smax = sb("smax", [P, 2, 2])
        nsmax = sb("nsmax", [P, 2, 2])
        ssum = sb("ssum", [P, 2, 2])
        srec = sb("srec", [P, 2, 2])
        iota_e = sb("iota_e", [P, EXPERTS])
        first_more = sb("first_more", [P, EXPERTS])
        iota_s = sb("iota_s", [P, SLOTS])
        number_a = sb("number_a", [P, 2 * TT])
        place = sb("place", [P, 2 * TT], I32)
        place_lo = sb("place_lo", [P, 2 * TT], I32)
        gates = sb("gates", [P, TT, 2])
        raw = sb("raw", [P, BLOCKS], I32)
        to_row = sb("to_row", [P, BLOCKS], I32)
        from_row = sb("from_row", [P, BLOCKS // 2], I32)
        upper = sb("upper", [P, 1])
        gather_index = [sb(f"gather_index{u}", [P, 1], I32) for u in range(2)]
        store_index = [[sb(f"store_index{u}{b}", [P, 1], I32) for b in "ab"] for u in range(2)]
        more = sb("more", [P, 1 + MORE_BLOCKS], I32)
        ps = ctx.enter_context(nc.psum_tensor("ps", [P, BANKS, HALF], F32))

        xt = area_x[:, :].rearrange("p (k s) -> p k s", k=KD)
        mixt = area_b[:, 0:4096].rearrange("p (k s) -> p k s", k=KD)
        qt = mixt
        at = area_b[:, 0:4 * (PAD + S)].rearrange("p (g s) -> p g s", g=4)
        ut = area_b[:, 4 * (PAD + S):4 * (PAD + S) + 4 * S].rearrange("p (g s) -> p g s", g=4)
        cgt = work[:, :, :].rearrange("p a (m s) -> p (a m) s", m=2)
        zct = area_e[:, 0:4 * (S + 2)].rearrange("p (m s) -> p m s", m=4)
        pt = area_x[:, :].rearrange("p (h m s) -> p h m s", h=HEADS, m=MT)
        vn = area_kv[:, 0:2048].rearrange("p (t c) -> p t c", t=TT)
        dt_ = area_kv[:, 2048:4096].rearrange("p (g s) -> p g s", g=4)
        kt = area_kv[:, 0:2048].rearrange("p (n m) -> p n m", n=KD)
        va = area_kv[:, 2048:4096].rearrange("p (m d) -> p m d", m=MT)
        wpool = area_e[:, 0:512].rearrange("p (g d) -> p g d", g=4)
        wst = area_e[:, 512:1024].rearrange("p (h i) -> p h i", h=SG_HEADS)
        bsp = area_e[:, 1024:1536].rearrange("p (h i) -> p h i", h=SG_HEADS)
        lnvg, lnvb = area_e[:, 1536:2048], area_e[:, 2048:2560]
        mem_rows = gb
        memt = area_e[:, 0:2048].rearrange("p (k m) -> p k m", k=KD)
        upto = area_b[:, 1024:2048].rearrange("p (a b) -> p a b", a=EXPERTS)
        upto_x = area_b[:, 2048:3072].rearrange("p (a b) -> p a b", a=EXPERTS)
        more_x = area_b[:, 3072:3072 + MORE_BLOCKS * EXPERTS].rearrange("p (a b) -> p a b", a=MORE_BLOCKS)
        flat = work[:, :, :].rearrange("p a b -> p (a b)")
        used = [0]

        def small(n):
            used[0] += n
            assert used[0] <= 2 * D
            return flat[:, used[0] - n:used[0]]

        logits = small(TT * NROUTE).rearrange("p (t n) -> p t n", t=TT)
        oh_g = small(TT * GROUPS).rearrange("p (t g) -> p t g", t=TT)
        cand_g = small(TT * GROUPS).rearrange("p (t g) -> p t g", t=TT)
        exp_g = small(TT * GROUPS).rearrange("p (t g) -> p t g", t=TT)
        lm = small(TT * EXPERTS).rearrange("p (t e) -> p t e", t=TT)
        cand = small(TT * EXPERTS).rearrange("p (t e) -> p t e", t=TT)
        oh = [small(TT * EXPERTS).rearrange("p (t e) -> p t e", t=TT) for _ in range(2)]
        chosen = small(TT * EXPERTS).rearrange("p (t e) -> p t e", t=TT)
        ranks = small(TT * EXPERTS + EXPERTS)
        rank_i = small(TT * EXPERTS).bitcast(I32).rearrange("p (t e) -> p t e", t=TT)
        rank_hi = small(TT * EXPERTS).bitcast(I32).rearrange("p (t e) -> p t e", t=TT)
        slot = small(TT * EXPERTS).rearrange("p (t e) -> p t e", t=TT)
        gmax, gmin, v0, v1, gsum, dexp, scr = (small(TT) for _ in range(7))
        extra_i = small(EXPERTS).bitcast(I32)
        extra, upto_n, base_n = small(EXPERTS), small(EXPERTS), small(EXPERTS)
        place_n = small(2 * TT)
        more_n = small(MORE_BLOCKS)
        iota_b = small(MORE_BLOCKS)
        at_slot = area_a[:, 0:2 * TT * P].rearrange("p (n s) -> p n s", n=2 * TT)
        at_block = area_a[:, 2 * TT * P:2 * TT * (P + BLOCKS)].rearrange("p (n b) -> p n b", n=2 * TT)
        xg = [area_b[:, 0:1024], area_b[:, 2048:3072]]
        xgt = area_b[:, 1024:2048].rearrange("p (k s) -> p k s", k=KD)
        silu_sb = [area_a[0:SLOTS, 512 * b:512 * b + 512] for b in range(2)]
        hid = [area_a[0:SLOTS, 1024 + 512 * b:1536 + 512 * b] for b in range(2)]
        hidt = [area_a[:, 2048 + 256 * b:2304 + 256 * b].rearrange("p (j s) -> p j s", j=4) for b in range(2)]
        ysb = [[area_a[:, 2560 + 512 * b:3072 + 512 * b] for b in range(2)],
               [area_b[:, 3072 + 512 * b:3584 + 512 * b] for b in range(2)]]
        y_pair = [area_b[:, 0:2048], area_b[:, 2048:4096]]
        y_slot = RAW + 2 * ((splits["cg", 1, 0][0] + 1) % 2)
        y_pair += [ring[:, y_slot, 0:2 * D], ring[:, y_slot, 2 * D:4 * D]]

        x_dram = [nc.dram_tensor(f"x_rows{l}", [S, D], F32, kind="Internal").ap() for l in range(DEPTH)]
        y_dram = [nc.dram_tensor(f"y_rows{l}", [4 * S, HALF], F32, kind="Internal").ap() for l in range(DEPTH)]

        landed = [sem(f"slot_landed{n}") for n in range(RING)]
        filled = [sem(f"bank_filled{n}") for n in range(BANKS)]
        drained = [sem(f"bank_drained{n}") for n in range(BANKS)]
        w_hi_set = sem("w_hi_set")
        w_lo_set = sem("w_lo_set")
        hi_set = sem("hi_set")
        mem_landed = sem("mem_landed")
        x_landed = [sem(f"x_landed{n}") for n in range(TT)]
        even_landed = sem("even_landed")
        rows_landed = sem("rows_landed")
        gb_landed = sem("gb_landed")
        router_landed = sem("router_landed")
        ident_set = sem("ident_set")
        pool_set = sem("pool_set")
        consts_set = sem("consts_set")
        mask_set = sem("mask_set")
        tril_set = sem("tril_set")
        dve_step = sem("dve_step")
        var_ready = sem("var_ready")
        rstd_ready = sem("rstd_ready")
        x_ready = sem("x_ready")
        vn_ready = sem("vn_ready")
        pooled = sem("pooled")
        smax_ready = sem("smax_ready")
        p_ready = sem("p_ready")
        gated = sem("gated")
        mixt_ready = sem("mixt_ready")
        chosen_ready = sem("chosen_ready")
        place_ready = sem("place_ready")
        gate_in_ready = sem("gate_in_ready")
        gate_exp_ready = sem("gate_exp_ready")
        rows_known = sem("rows_known")
        more_known = sem("more_known")
        xg_cleared = sem("xg_cleared")
        x_stored = sem("x_stored")
        y_landed = [sem(f"y_landed{t}") for t in range(TT)]
        x_scaled = sem("x_scaled")
        out_stored = sem("out_stored")
        pool_step = sem("pool_step")
        index_seen = sem("index_seen")
        gathered = [sem(f"gathered{u}") for u in range(2)]
        silu_done = sem("silu_done")
        index_ready = [[sem(f"index_ready{u}{b}") for b in "ab"] for u in range(2)]
        stored = [[sem(f"stored{u}{b}") for b in "ab"] for u in range(2)]

        main, rest = [], []
        for l in range(DEPTH):
            main.append(Signals(landed, filled, drained, gathered, silu_done, index_ready, stored, pool_step,
                                jobs["moe", l], moe_uses[l], l, 0, PAIRS))
            m = f"more{l}"
            rest.append(Signals([sem(f"{m}_landed{n}") for n in range(RING)],
                                [sem(f"{m}_filled{n}") for n in range(BANKS)],
                                [sem(f"{m}_drained{n}") for n in range(BANKS)],
                                [sem(f"{m}_gathered{u}") for u in range(2)], sem(f"{m}_silu"),
                                [[sem(f"{m}_index{u}{b}") for b in "ab"] for u in range(2)],
                                [[sem(f"{m}_stored{u}{b}") for b in "ab"] for u in range(2)],
                                sem(f"{m}_step"), BANKS, [0] * RING, 0, PAIRS, MORE_PAIRS))

        def wait_filled(eng, *name):
            eng.wait_ge(filled[jobs[name] % BANKS], jobs[name] // BANKS + 1)

        def wait_drained(eng, *name):
            eng.wait_ge(drained[jobs[name] % BANKS], jobs[name] // BANKS + 1)

        def bank(*name):
            return ps[:, jobs[name] % BANKS, :]

        def is_drained(*name):
            return drained[jobs[name] % BANKS], 1

        def tile_view(slot, k):
            return ring[:, slot, 0:k * (KD * HALF // k)].rearrange("p (k n) -> p k n", k=k)

        split_chunks = KD // SPLIT_HALVES

        def split_number(what, l, c):
            return splits[what, l, c][0]

        def wait_pair_free(eng, number):
            if number >= 2:
                last = next(j for n, j in splits.values() if n == number - 2)
                eng.wait_ge(filled[last % BANKS], last // BANKS + 1)

        block = ctx.enter_context(nc.Block())

        @block.sync
        def _(sp):
            def halves(w, cols):
                return w.rearrange("(k p) n -> p k n", p=P)[:, :, cols]

            def cut(c):
                return slice(c * HALF, (c + 1) * HALF)

            source = {}
            for c, what in enumerate(("pool_a", "gate_u", "gate_v")):
                source[what, 0, 0] = halves(w_in_even[0], cut(c))
            for c in range(2):
                source["mix", 0, c] = halves(w_out_even[0], cut(c))
                source["mix", 1, c] = halves(w_out_odd[0], cut(c))
                for n, what in enumerate(("bg", "cg", "z")):
                    source[what, 1, c] = halves(w_in_odd[0], cut(2 * n + c))
                for l in range(DEPTH):
                    for what, w in (("q", wq_x), ("k", wk_x), ("v", wv_x), ("wo", wo_x)):
                        source[what, l, c] = halves(w[l], cut(c))

            def wait_free(free):
                if free and free[0] == "filled":
                    sp.wait_ge(filled[free[1] % BANKS], free[1] // BANKS + 1)
                elif free:
                    sp.wait_ge(w_lo_set, SPLIT_HALVES * (free[1] + 1))

            def expert_rows(w, l, e, k):
                return w[l, bass.ds(e, 1)].rearrange("o (p k) n -> p (o k) n", k=k)

            def load_expert(l, sig, j, blocks):
                a, b = blocks
                w, e, k = ((w1, a, 8), (w3, a, 8), (w1, b, 8), (w3, b, 8), (w2, a, 4), (w2, b, 4))[j]
                slot = TILE_SLOT[j]
                sp.dma_start(tile_view(slot, k), expert_rows(w, l, e, k)).then_inc(sig.landed[slot], 16)

            def load_pair(l, sig, i, blocks):
                for j in range(PAIR_TILES):
                    sig.wait_filled(sp, TILE_LAST[j], i, before=1)
                    load_expert(l, sig, j, blocks)

            def wait_stored(sig):
                for u in range(2):
                    for b in range(2):
                        sp.wait_ge(sig.stored[u][b], 16 * (sig.stored0 + sig.rounds))

            def load_outputs(l):
                wait_stored(main[l])
                for t in range(TT):
                    sp.dma_start(y_pair[t], y_dram[l].rearrange("(t p r) n -> t p (r n)", p=P, r=4)[t]).then_inc(y_landed[t], 16)

            for t in range(TT):
                sp.dma_start(xs[:, t, :], x[0, t * P:(t + 1) * P, :]).then_inc(x_landed[t], 16)
            for n, (kind, name, _) in enumerate(stream):
                l = name[1]
                if n == 2:
                    sp.dma_start(mem_rows[:, :, :], mem[0].rearrange("(m p) d -> p m d", p=P)).then_inc(mem_landed, 16)
                if kind in ("split", "whole"):
                    slot, _, free = tile_slots[name]
                    wait_free(free)
                    sp.dma_start(tile_view(slot, KD), source[name]).then_inc(landed[slot], 16)
                    if name == ("cg", 1, 0):
                        load_outputs(0)
                elif kind == "moe":
                    wait_free(tile_slots[name][2])
                    load_expert(l, main[l], name[2], (0, 1))
                else:
                    with sp.Fori(1, PAIRS) as i:
                        load_pair(l, main[l], i, (2 * i, 2 * i + 1))
                    sp.wait_ge(more_known, l + 1)
                    count = sp.value_load(more[0:1, 0:1], min_val=0, max_val=MORE_BLOCKS - 1)
                    with sp.If(count > 0):
                        with sp.Fori(0, MORE_PAIRS) as i:
                            a = sp.value_load(more[0:1, bass.ds(2 * i + 1, 1)], min_val=0, max_val=EXPERTS - 1)
                            b = sp.value_load(more[0:1, bass.ds(2 * i + 2, 1)], min_val=0, max_val=EXPERTS - 1)
                            load_pair(l, rest[l], i, (a, b))
                        for j in set(TILE_LAST):
                            rest[l].wait_filled(sp, j, MORE_PAIRS - 1)
                        wait_stored(rest[l])
                    if l + 1 == DEPTH:
                        load_outputs(l)

        @block.tensor
        def _(pe):
            order = [0]

            def begin(*name):
                n = jobs[name]
                assert n == order[0], name
                order[0] += 1
                if n >= BANKS:
                    pe.wait_ge(drained[n % BANKS], n // BANKS)
                return ps[:, n % BANKS, :], filled[n % BANKS]

            def weights(what, l, c):
                slot, uses, _ = tile_slots[what, l, c]
                pe.wait_ge(landed[slot], 16 * uses)
                return tile_view(slot, KD)

            known = set()

            def split_product(name, tile, x_known, operands, w_low_last=False):
                number = split_number(*tile)
                dst, done = begin(*name)
                passes = ((0, 0), (1, 0), (0, 1)) if w_low_last else ((0, 0), (0, 1), (1, 0))
                for n, (x_low, w_low) in enumerate(passes):
                    if n == 0 or x_low:
                        x_known(x_low)
                    for k in range(KD):
                        if k % split_chunks == 0 and not x_low and (number, w_low, k) not in known:
                            known.add((number, w_low, k))
                            pe.wait_ge(w_lo_set if w_low else w_hi_set, SPLIT_HALVES * number + k // split_chunks + 1)
                        stationary, moving = operands(k, x_low, w_low)
                        mm = pe.matmul(dst, stationary, moving, start=(n == 0 and k == 0),
                                       stop=(n == 2 and k == KD - 1))
                mm.then_inc(done, 1)

            def columns(name, tile, m, x_known):
                turn = split_number(*tile) % 2
                split_product(name, tile, x_known, lambda k, x_low, w_low: (
                    (w_hi, w_lo)[w_low][turn][:, k, m * P:(m + 1) * P], (x_hi, x_lo)[x_low][:, k, :]))

            def rows(name, tile, parts_, t, x_known, w_low_last=False):
                turn = split_number(*tile) % 2
                split_product(name, tile, x_known, lambda k, x_low, w_low: (
                    parts_[x_low][:, k, t * P:(t + 1) * P], (w_hi, w_lo)[w_low][turn][:, k, :]), w_low_last)

            def xt_known(site):
                def wait(low):
                    if (site, low) in known:
                        return
                    known.add((site, low))
                    if not low:
                        pe.wait_ge(hi_set, highs_done["xt", site])
                    else:
                        for t in range(TT):
                            for g in range(2):
                                wait_drained(pe, "xt", site, t, g)
                return wait

            def transposes(name, pieces):
                dst, done = begin(*name)
                for q, piece in enumerate(pieces):
                    mm = pe.transpose(dst[:, q * P:(q + 1) * P], piece, ident[:, :])
                mm.then_inc(done, 1)

            def transpose_x(site, ts):
                for t in ts:
                    if site:
                        pe.wait_ge(x_ready, TT * (site - 1) + t + 1)
                    else:
                        pe.wait_ge(x_landed[t], 16)
                    for g in range(2):
                        transposes(("xt", site, t, g), [xs[:, t, (4 * g + q) * P:(4 * g + q + 1) * P] for q in range(4)])

            def wait_xt(site, ts=range(TT)):
                for t in ts:
                    for g in range(2):
                        wait_drained(pe, "xt", site, t, g)

            def rows_both(l, what, parts_, x_known):
                for t, c in ROWS_ORDER:
                    rows((what, l, t, c), (what, l, c), parts_, t, lambda low: x_known(low, t, c))

            def keys(l, c):
                w = weights("k", l, c)
                for j in range(2):
                    dst, done = begin("k", l, c, j)
                    for m in range(2):
                        n = 2 * j + m
                        for k in range(KD):
                            mm = pe.matmul(dst[:, m * MEM:(m + 1) * MEM], w[:, k, n * P:(n + 1) * P], memt[:, k, :],
                                           start=(k == 0), stop=(k == KD - 1))
                    mm.then_inc(done, 1)

            def values(l, c):
                w = weights("v", l, c)
                for m in range(MT):
                    dst, done = begin("v", l, c, m)
                    for k in range(KD):
                        mm = pe.matmul(dst, memt[:, k, m * P:(m + 1) * P], w[:, k, :], start=(k == 0), stop=(k == KD - 1))
                    mm.then_inc(done, 1)

            def even_mixer():
                for t in range(TT):
                    rows(("gate_v", t), ("gate_v", 0, 0), (x_hi, x_lo), t, xt_known(0), w_low_last=True)
                for what in ("pool_a", "gate_u"):
                    for m in range(4):
                        columns((what, m), (what, 0, 0), m, xt_known(0))
                pe.wait_ge(tril_set, 1)
                transposes(("wst",), [wst[:, h, :] for h in range(SG_HEADS)])
                for g in range(4):
                    pe.wait_ge(pooled, g + 1)
                    dst, done = begin("pool_y", g)
                    pe.matmul(dst, wpool[:, g, :], dt_[:, g, :], start=True, stop=True).then_inc(done, 1)
                pe.wait_ge(vn_ready, TT)
                wait_drained(pe, "wst")
                for h in range(SG_HEADS):
                    dst, done = begin("spatial", h)
                    for t in range(TT):
                        mm = pe.matmul(dst[:, t * P:(t + 1) * P], vn[:, t, h * P:(h + 1) * P], wst[:, h, :],
                                       start=True, stop=True)
                    mm.then_inc(done, 1)
                pe.wait_ge(mem_landed, 16)
                for m in range(MT):
                    for g in range(2):
                        transposes(("memt", m, g), [mem_rows[:, m, (4 * g + q) * P:(4 * g + q + 1) * P] for q in range(4)])

                def mixed(low, t, c):
                    if (t, c) != ROWS_ORDER[0]:
                        return
                    if not low:
                        pe.wait_ge(hi_set, highs_done["mix", 0])
                    else:
                        for g in range(4):
                            wait_drained(pe, "pool_y", g)
                        pe.wait_ge(mixt_ready, SG_HEADS)
                rows_both(0, "mix", (x_hi, x_lo), mixed)

            def odd_mixer():
                for c in range(2):
                    for what in ("cg", "z", "bg"):
                        for m in range(4):
                            columns((what, c, m), (what, 1, c), m, xt_known(3))

                def mixed(low, t, c):
                    if c == 0:
                        if not low:
                            pe.wait_ge(hi_set, highs_done["xt", 3] + t + 1)
                        else:
                            pe.wait_ge(mixt_ready, SG_HEADS + t + 1)
                rows_both(1, "mix", (x_hi, x_lo), mixed)

            def scores(l, j):
                t, hp = j // 2, j % 2
                dst, done = begin("s", l, j)
                for h in range(2):
                    for k in range(2):
                        n = 2 * (2 * hp + h) + k
                        mm = pe.matmul(dst[:, h * MEM:(h + 1) * MEM], qt[:, n, t * P:(t + 1) * P], kt[:, n, :],
                                       start=(k == 0), stop=(k == 1))
                mm.then_inc(done, 1)

            def attention(l):
                for c in range(2):
                    for m in range(4):
                        columns(("q", l, c, m), ("q", l, c), m, xt_known(3 * l + 1))
                for c in range(2):
                    for j in range(2):
                        wait_drained(pe, "k", l, c, j)
                    for m in range(4):
                        wait_drained(pe, "q", l, c, m)
                scores(l, 0)
                scores(l, 1)
                for j in range(8):
                    if j + 2 < 8:
                        scores(l, j + 2)
                    pe.wait_ge(p_ready, 8 * l + j + 1)
                    transposes(("pt", l, j), [work[:, j % 2, q * P:(q + 1) * P] for q in range(4)])
                for c in range(2):
                    for m in range(MT):
                        wait_drained(pe, "v", l, c, m)
                for j in range(8):
                    wait_drained(pe, "pt", l, j)
                for n in range(8):
                    dst, done = begin("o", l, n)
                    for m in range(MT):
                        mm = pe.matmul(dst, va[:, m, n * P:(n + 1) * P], pt[:, n // 2, m, :],
                                       start=(m == 0), stop=(m == MT - 1))
                    mm.then_inc(done, 1)

                def mixed(low, t, c):
                    if (t, c) != ROWS_ORDER[0]:
                        return
                    if not low:
                        pe.wait_ge(hi_set, highs_done["o", l])
                    else:
                        for n in range(8):
                            wait_drained(pe, "o", l, n)
                rows_both(l, "wo", (o_hi, o_lo), mixed)

            def route(l):
                wait_xt(3 * l + 2)
                pe.wait_ge(router_landed, 16 * 5 * (l + 1))
                dst, done = begin("route", l)
                for t in range(TT):
                    for k in range(KD):
                        mm = pe.matmul(dst[:, t * NROUTE:(t + 1) * NROUTE], xt[:, k, t * P:(t + 1) * P], wr[:, k, :],
                                       start=(k == 0), stop=(k == KD - 1))
                mm.then_inc(done, 1)

            def rank(l):
                pe.wait_ge(chosen_ready, l + 1)
                dst, done = begin("rank", l)
                for t in range(TT + 1):
                    cols = dst[:, t * EXPERTS:(t + 1) * EXPERTS]
                    for b in range(min(t, TT)):
                        mm = pe.matmul(cols, ones[:, :], chosen[:, b, :], start=(b == 0), stop=(b == TT - 1))
                    if t < TT:
                        mm = pe.matmul(cols, before[:, :], chosen[:, t, :], start=(t == 0), stop=True)
                mm.then_inc(done, 1)

            def slot_table(l):
                pe.wait_ge(place_ready, l + 1)
                dst, done = begin("table", l)
                for n in range(2 * TT):
                    mm = pe.matmul(dst[:, 0:BLOCKS], at_slot[:, n, :], at_block[:, n, :],
                                   start=(n == 0), stop=(n == 2 * TT - 1))
                mm.then_inc(done, 1)

            def pair(sig, u, i):
                p = 2 * i + u

                def tile(j, k):
                    slot = TILE_SLOT[j]
                    pe.wait_ge(sig.landed[slot], 16 * (sig.slot_uses[slot] + 1 + p))
                    return tile_view(slot, k)

                def bank_of(j):
                    sig.wait_drained(pe, j, p, before=1)
                    return ps[:, sig.bank(j), :]

                pe.wait_ge(sig.gathered[u], 16 * (sig.gathered0 + 1 + i))
                for j in (XG0, XG1):
                    dst = bank_of(j)
                    for q in range(4):
                        k = 4 * (j - XG0) + q
                        mm = pe.transpose(dst[:, q * P:(q + 1) * P], xg[u][:, k:D:KD], ident[:, :])
                    mm.then_inc(sig.filled[sig.bank(j)], 1)
                sig.wait_drained(pe, XG0, p)
                sig.wait_drained(pe, XG1, p)
                for b, j in enumerate((HA, HB)):
                    ws = [tile(2 * b, 8), tile(2 * b + 1, 8)]
                    dst = bank_of(j)
                    for k in range(KD):
                        for half in range(2):
                            mm = pe.matmul(dst[half * SLOTS:(half + 1) * SLOTS, :],
                                           xgt[:, k, b * SLOTS:(b + 1) * SLOTS], ws[half][:, k, :],
                                           start=(k == 0), stop=(k == KD - 1))
                    mm.then_inc(sig.filled[sig.bank(j)], 1)
                for b, (jh, jt, jy) in enumerate(((HA, TA, YA), (HB, TB, YB))):
                    pe.wait_ge(ident_set, 2)
                    sig.wait_drained(pe, jh, p)
                    dst = bank_of(jt)
                    for q in range(4):
                        mm = pe.transpose(dst[:, q * SLOTS:(q + 1) * SLOTS], hid[b][:, q * P:(q + 1) * P],
                                          ident[0:SLOTS, 0:SLOTS])
                    mm.then_inc(sig.filled[sig.bank(jt)], 1)
                    w = tile(4 + b, 4)
                    sig.wait_drained(pe, jt, p)
                    dst = bank_of(jy)
                    for q in range(4):
                        for half in range(2):
                            mm = pe.matmul(dst[half * SLOTS:(half + 1) * SLOTS, :], hidt[b][:, q, :],
                                           w[:, q, half * HALF:(half + 1) * HALF], start=(q == 0), stop=(q == 3))
                    mm.then_inc(sig.filled[sig.bank(jy)], 1)

            def experts(l):
                with pe.Fori(0, main[l].rounds) as i:
                    for u in range(2):
                        pair(main[l], u, i)
                order[0] += BANKS * PAIRS
                pe.wait_ge(more_known, l + 1)
                count = pe.value_load(more[0:1, 0:1], min_val=0, max_val=MORE_BLOCKS - 1)
                with pe.If(count > 0):
                    for j in range(BANKS):
                        main[l].wait_drained(pe, j, PAIRS - 1)
                    for n in range(BANKS):
                        pe.sem_inc(rest[l].filled[n], 1)
                        pe.sem_inc(rest[l].drained[n], 1)
                    with pe.Fori(0, rest[l].rounds) as i:
                        for u in range(2):
                            pair(rest[l], u, i)
                    for j in range(BANKS):
                        rest[l].wait_drained(pe, j, MORE_PAIRS - 1)

            pe.wait_ge(ident_set, 2)
            transpose_x(0, range(TT))
            for l in range(DEPTH):
                if l == 0:
                    even_mixer()
                else:
                    odd_mixer()
                if l == 0:
                    for m in range(MT):
                        for g in range(2):
                            wait_drained(pe, "memt", m, g)
                    for c in range(2):
                        keys(0, c)
                    for c in range(2):
                        values(0, c)
                transpose_x(3 * l + 1, range(TT))
                attention(l)
                transpose_x(3 * l + 2, range(TT - 1))
                if l == 0:
                    keys(1, 0)
                transpose_x(3 * l + 2, [TT - 1])
                route(l)
                if l == 0:
                    keys(1, 1)
                rank(l)
                if l == 0:
                    values(1, 0)
                slot_table(l)
                if l == 0:
                    values(1, 1)
                experts(l)
                if l + 1 < DEPTH:
                    transpose_x(3 * l + 3, range(TT))

        @block.scalar
        def _(act):
            def drain(name, dst, src, func=ACT.Copy, **how):
                wait_filled(act, *name)
                act.activation(dst, src, func, **how).then_inc(*is_drained(*name))

            def high(dst, src, func=ACT.Copy, **how):
                act.activation(dst, src, func, **how).then_inc(hi_set, 1)

            def high_xt(site):
                for t in range(TT):
                    for g in range(2):
                        wait_filled(act, "xt", site, t, g)
                        high(x_hi[:, 4 * g:4 * g + 4, t * P:(t + 1) * P],
                             bank("xt", site, t, g).rearrange("p (q s) -> p q s", q=4))

            def copy_xt(site, ts):
                for t in ts:
                    for g in range(2):
                        name = ("xt", site, t, g)
                        drain(name, xt[:, 4 * g:4 * g + 4, t * P:(t + 1) * P],
                              bank(*name).rearrange("p (q s) -> p q s", q=4))

            def split_weights(what, l, c):
                number = split_number(what, l, c)
                slot, uses, _ = tile_slots[what, l, c]
                wait_pair_free(act, number)
                act.wait_ge(landed[slot], 16 * uses)
                for n in range(SPLIT_HALVES):
                    ks = slice(n * split_chunks, (n + 1) * split_chunks)
                    act.activation(w_hi[number % 2][:, ks, :], tile_view(slot, KD)[:, ks, :], ACT.Copy).then_inc(w_hi_set, 1)

            def keys(l, c):
                for j in range(2):
                    n = 4 * c + 2 * j
                    drain(("k", l, c, j), kt[:, n:n + 2, :], bank("k", l, c, j).rearrange("p (q m) -> p q m", q=2))

            def values(l, c):
                for m in range(MT):
                    drain(("v", l, c, m), va[:, m, c * HALF:(c + 1) * HALF], bank("v", l, c, m))

            def even_mixer():
                split_weights("gate_v", 0, 0)
                split_weights("pool_a", 0, 0)
                for t in range(TT):
                    drain(("gate_v", t), vn[:, t, :], bank("gate_v", t), ACT.Gelu_apprx_tanh)
                split_weights("gate_u", 0, 0)
                for m in range(4):
                    drain(("pool_a", m), at[:, m, PAD:PAD + S], bank("pool_a", m))
                split_weights("mix", 0, 0)
                for m in range(4):
                    drain(("gate_u", m), ut[:, m, :], bank("gate_u", m), ACT.Gelu_apprx_tanh)
                drain(("wst",), wst[:, :, :], bank("wst").rearrange("p (h i) -> p h i", h=SG_HEADS))
                act.wait_ge(rows_landed, 16 * 5)
                for g in range(4):
                    wait_filled(act, "pool_y", g)
                    high(x_hi[:, g, :], bank("pool_y", g), scale=pscale[:, g:g + 1])
                for h in range(SG_HEADS):
                    act.wait_ge(gated, h + 1)
                    high(x_hi[:, 4 + h, :], work[:, h % 2, 0:S])
                split_weights("mix", 0, 1)
                for m in range(MT):
                    for g in range(2):
                        drain(("memt", m, g), memt[:, 4 * g:4 * g + 4, m * P:(m + 1) * P],
                              bank("memt", m, g).rearrange("p (q s) -> p q s", q=4))

            def odd_mixer():
                split_weights("z", 1, 0)
                for c in range(2):
                    for m in range(4):
                        if c:
                            wait_drained(act, "z", 0, m)
                        drain(("cg", c, m), cgt[:, m, :], bank("cg", c, m))
                    split_weights("bg", 1, c)
                    split_weights(*(("mix", 1, 0) if c else ("cg", 1, 1)))
                    if not c:
                        split_weights("z", 1, 1)
                for m in range(4):
                    wait_drained(act, "bg", 1, m)
                for t in range(TT):
                    high(x_hi[:, :, t * P:(t + 1) * P], mixt[:, :, t * P:(t + 1) * P])
                split_weights("mix", 1, 1)
                split_weights("q", 1, 0)

            def attention(l):
                split_weights("q", l, 1)
                for m in range(4):
                    drain(("q", l, 0, m), qt[:, m, :], bank("q", l, 0, m))
                split_weights("wo", l, 0)
                for m in range(4):
                    drain(("q", l, 1, m), qt[:, 4 + m, :], bank("q", l, 1, m))

                def exps(j):
                    act.wait_ge(smax_ready, 8 * l + j + 1)
                    for h in range(2):
                        e = act.activation(work[:, j % 2, h * MEM:(h + 1) * MEM], bank("s", l, j)[:, h * MEM:(h + 1) * MEM],
                                           ACT.Exp, bias=nsmax[:, j % 2, h:h + 1], scale=SCALE,
                                           accum_out=ssum[:, j % 2, h:h + 1])
                    e.then_inc(*is_drained("s", l, j))

                exps(0)
                exps(1)
                for j in range(8):
                    t, hp = j // 2, j % 2
                    drain(("pt", l, j), pt[:, 2 * hp:2 * hp + 2, :, t * P:(t + 1) * P],
                          bank("pt", l, j).rearrange("p (h m s) -> p h m s", h=2, m=MT))
                    if j + 2 < 8:
                        exps(j + 2)
                for n in range(8):
                    wait_filled(act, "o", l, n)
                    high(o_hi[:, n, :], bank("o", l, n))
                split_weights("wo", l, 1)

            def pair(sig, u, i):
                p = 2 * i + u
                for j in (XG0, XG1):
                    sig.wait_filled(act, j, p)
                    g = 4 * (j - XG0)
                    act.activation(xgt[:, g:g + 4, :], ps[:, sig.bank(j), :].rearrange("p (q s) -> p q s", q=4),
                                   ACT.Copy).then_inc(sig.drained[sig.bank(j)], 1)
                for b, j in enumerate((HA, HB)):
                    sig.wait_filled(act, j, p)
                    act.activation(silu_sb[b], ps[0:SLOTS, sig.bank(j), :], ACT.Silu).then_inc(sig.silu, 1)
                for b, j in enumerate((TA, TB)):
                    sig.wait_filled(act, j, p)
                    act.activation(hidt[b], ps[:, sig.bank(j), 0:4 * SLOTS].rearrange("p (q s) -> p q s", q=4),
                                   ACT.Copy).then_inc(sig.drained[sig.bank(j)], 1)

            def experts(l):
                with act.Fori(0, main[l].rounds) as i:
                    for u in range(2):
                        pair(main[l], u, i)
                act.wait_ge(more_known, l + 1)
                count = act.value_load(more[0:1, 0:1], min_val=0, max_val=MORE_BLOCKS - 1)
                with act.If(count > 0):
                    with act.Fori(0, rest[l].rounds) as i:
                        for u in range(2):
                            pair(rest[l], u, i)

            for l in range(DEPTH):
                high_xt(3 * l)
                if l == 0:
                    even_mixer()
                    for c in range(2):
                        keys(0, c)
                    values(0, 0)
                    split_weights("q", 0, 0)
                    values(0, 1)
                else:
                    odd_mixer()
                high_xt(3 * l + 1)
                attention(l)
                copy_xt(3 * l + 2, range(TT - 1))
                if l == 0:
                    keys(1, 0)
                copy_xt(3 * l + 2, [TT - 1])
                if l == 0:
                    keys(1, 1)
                act.wait_ge(gate_in_ready, l + 1)
                act.activation(exp_g[:, :, :], exp_g[:, :, :], ACT.Exp).then_inc(gate_exp_ready, 1)
                act.activation(dexp, dexp, ACT.Exp).then_inc(gate_exp_ready, 1)
                if l == 0:
                    values(1, 0)
                    values(1, 1)
                experts(l)
                if l + 1 < DEPTH:
                    split_weights("cg", 1, 0)
                act.wait_ge(x_stored, 16 * TT * (l + 1))
                for t in range(TT):
                    act.activation(xs[:, t, :], xs[:, t, :], ACT.Copy, scale=ALPHA).then_inc(x_scaled, 1)

        @block.vector
        def _(dve):
            steps = [0]
            norms = [0]

            def link(ins):
                steps[0] += 1
                ins.then_inc(dve_step, 1)
                dve.wait_ge(dve_step, steps[0])

            def measure(parts):
                turn = norms[0] % 2
                for n, part in enumerate(parts):
                    st = dve.bn_stats(stats[:, 6 * n:6 * n + 6], part)
                link(st)
                link(dve.bn_aggr(mean_var[turn][:, :], stats[:, 0:6 * len(parts)]))
                dve.tensor_scalar(var_eps[turn][:, :], mean_var[turn][:, 1:2], LN_EPS, None, ALU.add).then_inc(var_ready, 1)
                norms[0] += 1
                return norms[0]

            def normalize(row, norm):
                turn = (norm - 1) % 2
                dve.wait_ge(rstd_ready, norm)
                link(dve.tensor_scalar(row, row, mean_var[turn][:, 0:1], rstd[turn][:, 0:1], ALU.subtract, ALU.mult))

            highs = [0]

            def low(hi, lo, src):
                highs[0] += 1
                dve.wait_ge(hi_set, highs[0])
                return dve.tensor_tensor(lo, src, hi.bitcast(F32), ALU.subtract)

            def low_xt(site, t):
                for g in range(2):
                    cols = (slice(None), slice(4 * g, 4 * g + 4), slice(t * P, (t + 1) * P))
                    low(x_hi[cols], x_lo[cols], bank("xt", site, t, g).rearrange("p (q s) -> p q s", q=4))\
                        .then_inc(*is_drained("xt", site, t, g))

            def split_weights(what, l, c):
                number = split_number(what, l, c)
                slot, uses, _ = tile_slots[what, l, c]
                wait_pair_free(dve, number)
                for n in range(SPLIT_HALVES):
                    ks = slice(n * split_chunks, (n + 1) * split_chunks)
                    dve.wait_ge(w_hi_set, SPLIT_HALVES * number + n + 1)
                    dve.tensor_tensor(w_lo[number % 2][:, ks, :], tile_view(slot, KD)[:, ks, :],
                                      w_hi[number % 2][:, ks, :].bitcast(F32), ALU.subtract).then_inc(w_lo_set, 1)

            def layer_norm(site, residual, ahead, between=lambda t: None):
                def begin(t):
                    row = work[:, t % 2, :]
                    residual(t, row)
                    return measure([row[:, 0:512], row[:, 512:D]])

                def end(t, norm):
                    row = work[:, t % 2, :]
                    turn = (norm - 1) % 2
                    if t == 0:
                        dve.wait_ge(gb_landed, 32 * (site + 1))
                    link(dve.scalar_tensor_tensor(out=row, in0=row, scalar=mean_var[turn][:, 0:1], in1=gb[:, 0, :],
                                                  op0=ALU.subtract, op1=ALU.mult))
                    dve.wait_ge(rstd_ready, norm)
                    dve.scalar_tensor_tensor(out=xs[:, t, :], in0=row, scalar=rstd[turn][:, 0:1], in1=gb[:, 1, :],
                                             op0=ALU.mult, op1=ALU.add).then_inc(x_ready, 1)

                norm = begin(0)
                for t in range(1, TT):
                    if ahead:
                        if t >= 2:
                            dve.wait_ge(x_ready, TT * site + t - 1)
                        following = begin(t)
                        end(t - 1, norm)
                        norm = following
                    else:
                        end(t - 1, norm)
                        between(t)
                        norm = begin(t)
                end(TT - 1, norm)
                dve.wait_ge(x_ready, TT * (site + 1))

            def from_banks(what, l):
                def residual(t, row):
                    for c in range(2):
                        wait_filled(dve, what, l, t, c)
                        cols = slice(c * HALF, (c + 1) * HALF)
                        dve.scalar_tensor_tensor(out=row[:, cols], in0=xs[:, t, cols], scalar=ALPHA,
                                                 in1=bank(what, l, t, c), op0=ALU.mult, op1=ALU.add)\
                           .then_inc(*is_drained(what, l, t, c))
                    for c in range(2):
                        wait_drained(dve, what, l, t, c)
                return residual

            def from_experts(l):
                def residual(t, row):
                    dve.wait_ge(y_landed[t], 16 * (l + 1))
                    dve.wait_ge(x_scaled, TT * l + t + 1)
                    link(dve.scalar_tensor_tensor(out=row, in0=y_pair[t][:, 0:D], scalar=gates[:, t, 0:1], in1=xs[:, t, :],
                                                  op0=ALU.mult, op1=ALU.add))
                    link(dve.scalar_tensor_tensor(out=row, in0=y_pair[t][:, D:2 * D], scalar=gates[:, t, 1:2], in1=row,
                                                  op0=ALU.mult, op1=ALU.add))
                return residual

            def even_mixer():
                link(dve.memset(at[:, :, 0:PAD], 0.0))
                for n in range(PAD):
                    c = dve.memset(inv_count[:, n:n + 1], 1.0 / (n + 1))
                link(c)
                dve.wait_ge(rows_landed, 16 * 5)
                for t in range(TT):
                    wait_drained(dve, "gate_v", t)
                    v = vn[:, t, :]
                    normalize(v, measure([v]))
                    link(dve.tensor_tensor(v, v, lnvg, ALU.mult))
                    dve.tensor_tensor(v, v, lnvb, ALU.add).then_inc(vn_ready, 1)
                split_weights("gate_u", 0, 0)
                for g, w in enumerate(WINDOWS):
                    wait_drained(dve, "pool_a", g)
                    src, span, turn = at[:, g, :], 1, 0
                    while span < w:
                        dst = work[:, turn, 0:PAD + S]
                        link(dve.tensor_tensor(dst[:, 2 * span - 1:], src[:, 2 * span - 1:], src[:, span - 1:PAD + S - span], ALU.add))
                        src, span, turn = dst, 2 * span, 1 - turn
                    a = at[:, g, PAD:]
                    link(dve.scalar_tensor_tensor(out=dt_[:, g, :], in0=src[:, PAD:], scalar=1.0 / w, in1=a,
                                                  op0=ALU.mult, op1=ALU.subtract))
                    head = src[:, PAD:PAD + w - 1]
                    link(dve.tensor_tensor(head, head, inv_count[:, 0:w - 1], ALU.mult))
                    dve.tensor_tensor(dt_[:, g, 0:w - 1], head, a[:, 0:w - 1], ALU.subtract).then_inc(pooled, 1)
                    dve.wait_ge(pooled, g + 1)
                split_weights("mix", 0, 0)
                for g in range(4):
                    highs[0] += 1
                    dve.wait_ge(hi_set, highs[0])
                    dve.scalar_tensor_tensor(out=x_lo[:, g, :], in0=bank("pool_y", g), scalar=pscale[:, g:g + 1],
                                             in1=x_hi[:, g, :].bitcast(F32), op0=ALU.mult, op1=ALU.subtract)\
                        .then_inc(*is_drained("pool_y", g))

                def low_gated(h):
                    low(x_hi[:, 4 + h, :], x_lo[:, 4 + h, :], work[:, h % 2, 0:S]).then_inc(mixt_ready, 1)

                for h in range(SG_HEADS):
                    wait_filled(dve, "spatial", h)
                    if h >= 2:
                        dve.wait_ge(mixt_ready, h - 1)
                    gate = work[:, h % 2, 0:S]
                    dve.tensor_tensor(gate.rearrange("p (t i) -> p t i", t=TT),
                                      bank("spatial", h).rearrange("p (t i) -> p t i", t=TT),
                                      bsp[:, h:h + 1, :].broadcast_to([P, TT, P]), ALU.add)\
                       .then_inc(*is_drained("spatial", h))
                    wait_drained(dve, "spatial", h)
                    wait_drained(dve, "gate_u", h)
                    dve.tensor_tensor(gate, gate, ut[:, h, :], ALU.mult).then_inc(gated, 1)
                    if h:
                        low_gated(h - 1)
                low_gated(SG_HEADS - 1)
                split_weights("mix", 0, 1)

            def odd_mixer():
                split_weights("z", 1, 0)
                link(dve.memset(zct[:, :, 0:2], 0.0))
                for c in range(2):
                    split_weights("bg", 1, c)
                    for m in range(4):
                        wait_filled(dve, "z", c, m)
                        wait_drained(dve, "cg", c, m)
                        dve.tensor_tensor(zct[:, m, 2:], bank("z", c, m), cgt[:, m, :], ALU.mult)\
                           .then_inc(*is_drained("z", c, m))
                    split_weights(*(("mix", 1, 0) if c else ("cg", 1, 1)))
                    for m in range(4):
                        n = 4 * c + m
                        wait_drained(dve, "z", c, m)
                        conv = mixt[:, n, :]
                        link(dve.tensor_scalar(conv, zct[:, m, 0:S], convw[:, n, 0:1], convb[:, n:n + 1], ALU.mult, ALU.add))
                        for tap in (1, 2):
                            link(dve.scalar_tensor_tensor(out=conv, in0=zct[:, m, tap:tap + S], scalar=convw[:, n, tap:tap + 1],
                                                          in1=conv, op0=ALU.mult, op1=ALU.add))
                        wait_filled(dve, "bg", c, m)
                        dve.tensor_tensor(conv, bank("bg", c, m), conv, ALU.mult).then_inc(*is_drained("bg", c, m))
                        wait_drained(dve, "bg", c, m)
                    if not c:
                        split_weights("z", 1, 1)
                for t in range(TT):
                    cols = (slice(None), slice(None), slice(t * P, (t + 1) * P))
                    low(x_hi[cols], x_lo[cols], mixt[cols]).then_inc(mixt_ready, 1)
                split_weights("mix", 1, 1)

            def attention(l):
                def find_max(j):
                    wait_filled(dve, "s", l, j)
                    link(dve.tensor_reduce(smax[:, j % 2, :], bank("s", l, j).rearrange("p (h m) -> p h m", h=2), AX.X, ALU.max))
                    dve.tensor_scalar(nsmax[:, j % 2, :], smax[:, j % 2, :], -SCALE, None, ALU.mult).then_inc(smax_ready, 1)

                split_weights("q", l, 1)
                split_weights("wo", l, 0)
                find_max(0)
                find_max(1)
                for j in range(8):
                    wait_drained(dve, "s", l, j)
                    link(dve.reciprocal(srec[:, j % 2, :], ssum[:, j % 2, :]))
                    for h in range(2):
                        p = work[:, j % 2, h * MEM:(h + 1) * MEM]
                        s = dve.tensor_scalar(p, p, srec[:, j % 2, h:h + 1], None, ALU.mult)
                    s.then_inc(p_ready, 1)
                    if j + 2 < 8:
                        find_max(j + 2)
                for n in range(8):
                    low(o_hi[:, n, :], o_lo[:, n, :], bank("o", l, n)).then_inc(*is_drained("o", l, n))
                split_weights("wo", l, 1)

            def first_of(cands, values, top, iota, least, onehot):
                shape = list(values.shape)
                link(dve.tensor_tensor(cands, values, top.unsqueeze(2).broadcast_to(shape), ALU.is_equal))
                link(dve.scalar_tensor_tensor(out=cands, in0=cands, scalar=-100.0, in1=iota.unsqueeze(1).broadcast_to(shape),
                                              op0=ALU.mult, op1=ALU.add))
                link(dve.tensor_reduce(least, cands, AX.X, ALU.min))
                link(dve.tensor_tensor(onehot, cands, least.unsqueeze(2).broadcast_to(shape), ALU.is_equal))

            def router(l):
                wait_filled(dve, "route", l)
                dve.tensor_tensor(logits, bank("route", l)[:, 0:TT * NROUTE].rearrange("p (t n) -> p t n", t=TT),
                                  br[:, :].unsqueeze(1).broadcast_to([P, TT, NROUTE]), ALU.add)\
                   .then_inc(*is_drained("route", l))
                wait_drained(dve, "route", l)
                lg = logits[:, :, 0:GROUPS]
                link(dve.tensor_reduce(gmax, lg, AX.X, ALU.max))
                first_of(cand_g, lg, gmax, iota_e[:, 0:GROUPS], gmin, oh_g)
                link(dve.tensor_tensor(exp_g, lg, gmax.unsqueeze(2).broadcast_to([P, TT, GROUPS]), ALU.subtract))
                link(dve.tensor_scalar(oh_g, oh_g, -1.0, BIG, ALU.add, ALU.mult))
                link(dve.tensor_tensor(lm.rearrange("p t (g e) -> p t g e", g=GROUPS),
                                       logits[:, :, GROUPS:].rearrange("p t (g e) -> p t g e", g=GROUPS),
                                       oh_g.unsqueeze(3).broadcast_to([P, TT, GROUPS, PER_GROUP]), ALU.add))
                link(dve.tensor_reduce(v0, lm, AX.X, ALU.max))
                first_of(cand, lm, v0, iota_e[:, :], scr, oh[0])
                link(dve.scalar_tensor_tensor(out=lm, in0=oh[0], scalar=-3 * BIG, in1=lm, op0=ALU.mult, op1=ALU.add))
                link(dve.tensor_reduce(v1, lm, AX.X, ALU.max))
                first_of(cand, lm, v1, iota_e[:, :], scr, oh[1])
                dve.tensor_tensor(chosen, oh[0], oh[1], ALU.add).then_inc(chosen_ready, 1)
                dve.tensor_tensor(dexp, v1, v0, ALU.subtract).then_inc(gate_in_ready, 1)

                dve.memset(xg[0], 0.0).then_inc(xg_cleared, 1)

                wait_filled(dve, "rank", l)
                dve.tensor_copy(ranks, bank("rank", l)[:, 0:(TT + 1) * EXPERTS]).then_inc(*is_drained("rank", l))
                wait_drained(dve, "rank", l)
                rank_t = ranks[:, 0:TT * EXPERTS].rearrange("p (t e) -> p t e", t=TT)
                link(dve.tensor_copy(rank_i, rank_t))
                link(dve.tensor_scalar(extra_i, ranks[:, TT * EXPERTS:], float(SLOTS - 1), None, ALU.add))
                shift = SLOTS.bit_length() - 1
                link(dve.tensor_scalar(rank_hi, rank_i, shift, None, ALU.logical_shift_right))
                link(dve.tensor_scalar(rank_i, rank_i, SLOTS - 1, None, ALU.bitwise_and))
                link(dve.tensor_scalar(extra_i, extra_i, shift, None, ALU.logical_shift_right))
                link(dve.tensor_scalar(extra, extra_i, -1.0, 0.0, ALU.add, ALU.max))
                dve.wait_ge(mask_set, 2 * (l + 1))
                link(dve.tensor_tensor(upto_x, upto, extra.unsqueeze(1).broadcast_to([P, EXPERTS, EXPERTS]), ALU.mult))
                link(dve.tensor_reduce(upto_n, upto_x, AX.X, ALU.add))
                link(dve.tensor_tensor(base_n, upto_n, extra, ALU.subtract))
                link(dve.tensor_tensor(base_n, base_n, first_more[:, :], ALU.add))
                rows = [P, TT, EXPERTS]
                link(dve.scalar_tensor_tensor(out=slot, in0=rank_hi, scalar=0.0, in1=base_n.unsqueeze(1).broadcast_to(rows),
                                              op0=ALU.is_gt, op1=ALU.mult))
                link(dve.tensor_tensor(slot, slot, rank_hi, ALU.add))
                link(dve.tensor_tensor(slot, slot, iota_e[:, :].unsqueeze(1).broadcast_to(rows), ALU.add))
                link(dve.scalar_tensor_tensor(out=slot, in0=rank_i, scalar=float(SLOTS), in1=slot, op0=ALU.mult, op1=ALU.add))
                for c in range(2):
                    link(dve.tensor_tensor(cand, oh[c], slot, ALU.mult))
                    link(dve.tensor_reduce(place_n[:, c * TT:(c + 1) * TT], cand, AX.X, ALU.add))
                link(dve.tensor_copy(place[:, :], place_n))
                link(dve.tensor_scalar(place_lo[:, :], place[:, :], SLOTS - 1, None, ALU.bitwise_and))
                link(dve.tensor_scalar(place[:, :], place[:, :], shift, None, ALU.logical_shift_right))
                half = [P, 2 * TT, SLOTS]
                for h in range(2):
                    dve.tensor_tensor(at_slot[:, :, h * SLOTS:(h + 1) * SLOTS], place[:, :].unsqueeze(2).broadcast_to(half),
                                      iota_s[:, :].unsqueeze(1).broadcast_to(half), ALU.is_equal)
                wide = [P, 2 * TT, BLOCKS]
                link(dve.tensor_tensor(at_block, place_lo[:, :].unsqueeze(2).broadcast_to(wide),
                                       iota_s[:, 0:BLOCKS].unsqueeze(1).broadcast_to(wide), ALU.is_equal))
                dve.tensor_tensor(at_block, at_block, number_a[:, :].unsqueeze(2).broadcast_to(wide), ALU.mult)\
                   .then_inc(place_ready, 1)

                dve.memset(xg[1], 0.0).then_inc(xg_cleared, 1)

                wait_filled(dve, "table", l)
                dve.tensor_scalar(raw[:, :], bank("table", l)[:, 0:BLOCKS], float(INVALID), None, ALU.add)\
                   .then_inc(*is_drained("table", l))
                wait_drained(dve, "table", l)
                dve.tensor_scalar(from_row[0:SLOTS, :], raw[0:SLOTS, 0:BLOCKS:2], 1, None, ALU.logical_shift_right)\
                   .then_inc(rows_known, 1)
                dve.tensor_scalar(from_row[SLOTS:P, :], raw[SLOTS:P, 1:BLOCKS:2], 1, None, ALU.logical_shift_right)\
                   .then_inc(rows_known, 1)
                dve.tensor_scalar(to_row[:, :], raw[:, :], 2.0, upper[:, 0:1], ALU.mult, ALU.add).then_inc(rows_known, 1)

                shape = [P, MORE_BLOCKS, EXPERTS]
                link(dve.tensor_tensor(more_x, upto_n.unsqueeze(1).broadcast_to(shape), iota_b.unsqueeze(2).broadcast_to(shape), ALU.is_le))
                link(dve.tensor_reduce(more_n, more_x, AX.X, ALU.add))
                link(dve.tensor_copy(more[:, 0:1], upto_n[:, EXPERTS - 1:EXPERTS]))
                dve.tensor_scalar(more[:, 1:], more_n, float(EXPERTS - 1), None, ALU.min).then_inc(more_known, 1)

                dve.wait_ge(gate_exp_ready, 2 * (l + 1))
                link(dve.tensor_reduce(gsum, exp_g, AX.X, ALU.add))
                link(dve.scalar_tensor_tensor(out=gsum, in0=dexp, scalar=1.0, in1=gsum, op0=ALU.add, op1=ALU.mult))
                link(dve.reciprocal(scr, gsum))
                link(dve.tensor_copy(gates[:, :, 0:1], scr.unsqueeze(2)))
                link(dve.tensor_tensor(gates[:, :, 1:2], scr.unsqueeze(2), dexp.unsqueeze(2), ALU.mult))

            def pair(sig, u, i):
                p = 2 * i + u
                for b, j in enumerate((HA, HB)):
                    dve.wait_ge(sig.silu, sig.silu0 + 2 * p + b + 1)
                    dve.tensor_tensor(hid[b].rearrange("s (q p) -> s p q", q=4),
                                      silu_sb[b].rearrange("s (p q) -> s p q", q=4),
                                      ps[SLOTS:P, sig.bank(j), :].rearrange("s (p q) -> s p q", q=4), ALU.mult)\
                       .then_inc(sig.drained[sig.bank(j)], 1)
                for b, j in enumerate((YA, YB)):
                    dve.wait_ge(sig.index_ready[u][b], sig.index0[u] + i + 1)
                    sig.wait_filled(dve, j, p)
                    dve.tensor_copy(ysb[u][b], ps[:, sig.bank(j), :]).then_inc(sig.drained[sig.bank(j)], 1)

            def experts(l):
                with dve.Fori(0, main[l].rounds) as i:
                    for u in range(2):
                        pair(main[l], u, i)
                dve.wait_ge(more_known, l + 1)
                count = dve.value_load(more[0:1, 0:1], min_val=0, max_val=MORE_BLOCKS - 1)
                with dve.If(count > 0):
                    with dve.Fori(0, rest[l].rounds) as i:
                        for u in range(2):
                            pair(rest[l], u, i)

            for t in range(TT):
                low_xt(0, t)
            split_weights("gate_v", 0, 0)
            split_weights("pool_a", 0, 0)
            for l in range(DEPTH):
                dve.wait_ge(consts_set, 1)
                if l == 0:
                    even_mixer()
                    layer_norm(3 * l, from_banks("mix", l), ahead=False)
                    split_weights("q", 0, 0)
                else:
                    odd_mixer()
                    layer_norm(3 * l, from_banks("mix", l), ahead=False,
                               between=lambda t: split_weights("q", 1, 0) if t == 2 else None)
                for t in range(TT):
                    low_xt(3 * l + 1, t)
                attention(l)
                layer_norm(3 * l + 1, from_banks("wo", l), ahead=False)
                router(l)
                experts(l)
                if l + 1 < DEPTH:
                    split_weights("cg", 1, 0)
                    layer_norm(3 * l + 2, from_experts(l), ahead=True)
                    for t in range(TT):
                        low_xt(3 * l + 3, t)
                else:
                    layer_norm(3 * l + 2, from_experts(l), ahead=True)

        @block.gpsimd
        def _(pool):
            sets = [0]
            norms = [0]

            def link(ins):
                sets[0] += 1
                ins.then_inc(pool_set, 1)
                pool.wait_ge(pool_set, sets[0])

            def powers(n):
                for _ in range(n):
                    turn = norms[0] % 2
                    norms[0] += 1
                    pool.wait_ge(var_ready, norms[0])
                    pool.tensor_tensor(rstd[turn][:, :], var_eps[turn][:, :], minus_half[:, :], ALU.pow).then_inc(rstd_ready, 1)

            def load_gb(site):
                if site:
                    pool.wait_ge(x_ready, TT * site)
                else:
                    for m in range(MT):
                        for g in range(2):
                            wait_filled(pool, "memt", m, g)
                l, n = site // 3, site % 3
                for c, v in enumerate((ln_g, ln_b)):
                    pool.dma_start(gb[:, c, :], v[l, n:n + 1, :].partition_broadcast(P)).then_inc(gb_landed, 16)

            def load_router(l):
                for g in range(GROUPS):
                    at_ = GROUPS + g * PER_GROUP
                    pool.dma_start(wr[:, :, at_:at_ + PER_GROUP], wr_expert[l, g].rearrange("(k p) e -> p k e", p=P))\
                        .then_inc(router_landed, 16)
                pool.dma_start(wr[:, :, 0:GROUPS], wr_group[l].rearrange("(k p) g -> p k g", p=P)).then_inc(router_landed, 16)

            def load_biases(l):
                pool.dma_start(br[:, 0:GROUPS], br_group[l:l + 1, :].partition_broadcast(P)).then_inc(rows_landed, 16)
                pool.dma_start(br[:, GROUPS:], br_expert[l:l + 1].rearrange("o g e -> o (g e)").partition_broadcast(P))\
                    .then_inc(rows_landed, 16)

            def masks(l):
                wait_filled(pool, "wo", l, TT - 1, 1)
                link(pool.memset(upto, 1.0))
                pool.affine_select(out=upto, in_=upto, compare_op=ALU.is_ge, fill=0.0, base=0,
                                   pattern=[[1, EXPERTS], [-1, EXPERTS]], channel_multiplier=0).then_inc(mask_set, 1)
                pool.wait_ge(x_ready, TT * (3 * l + 2))
                pool.iota(iota_b, [[1, MORE_BLOCKS]], base=0, channel_multiplier=0,
                          allow_small_or_imprecise_dtypes=True).then_inc(mask_set, 1)

            def dispatch(l):
                for t in range(TT):
                    pool.dma_start(x_dram[l][t * P:(t + 1) * P, :], xs[:, t, :]).then_inc(x_stored, 16)
                pool.wait_ge(rows_known, 3 * (l + 1))
                pool.wait_ge(x_stored, 16 * TT * (l + 1))
                pool.wait_ge(xg_cleared, 2 * (l + 1))

            last_row = pool.to_reg(S - 1)
            last_half = pool.to_reg(4 * S - 1)

            def gather(l, sig, u, p, step):
                pool.tensor_copy(gather_index[u][:, :], from_row[:, bass.ds(p, 1)]).then_inc(sig.pool_step, 1)
                pool.wait_ge(sig.pool_step, step)
                pool.sem_inc(index_seen, 1)
                pool.indirect_dma_start(xg[u], None, x_dram[l], bass.IndirectOffsetOnAxis(ap=gather_index[u][:, 0:1], axis=0),
                                        bounds_check=last_row, oob_is_err=False).then_inc(sig.gathered[u], 16)

            def set_index(sig, u, b, p):
                pool.tensor_copy(store_index[u][b][:, :], to_row[:, bass.ds(2 * p + b, 1)])\
                    .then_inc(sig.index_ready[u][b], 1)

            def step(l, sig, u, i):
                p = 2 * i + u
                sig.wait_filled(pool, XG1, p)
                pool.wait_ge(sig.gathered[u], 16 * (sig.gathered0 + 1 + i))
                gather(l, sig, u, p + (sig.pair0 + 2), p + (sig.step0 + 3))
                for b in range(2):
                    if u or sig.stored0 or not isinstance(i, int):
                        pool.wait_ge(sig.stored[1 - u][b], 16 * (sig.stored0 + i + u))
                    set_index(sig, 1 - u, b, p + (sig.pair0 + 1))
                for b, j in enumerate((YA, YB)):
                    sig.wait_drained(pool, j, p)
                    pool.wait_ge(sig.index_ready[u][b], sig.index0[u] + 1 + i)
                    pool.sem_inc(index_seen, 1)
                    pool.indirect_dma_start(y_dram[l], bass.IndirectOffsetOnAxis(ap=store_index[u][b][:, 0:1], axis=0),
                                            ysb[u][b], None, bounds_check=last_half, oob_is_err=False)\
                        .then_inc(sig.stored[u][b], 16)

            def pairs(l, sig):
                for u in range(2):
                    gather(l, sig, u, sig.pair0 + u, sig.step0 + u + 1)
                for b in range(2):
                    set_index(sig, 0, b, sig.pair0)
                for u in range(2):
                    step(l, sig, u, 0)
                with pool.Fori(1, sig.rounds) as i:
                    for u in range(2):
                        step(l, sig, u, i)
                for u in range(2):
                    pool.wait_ge(sig.gathered[u], 16 * (sig.gathered0 + 1 + sig.rounds))
                    for b in range(2):
                        pool.wait_ge(sig.stored[u][b], 16 * (sig.stored0 + sig.rounds))
                        pool.wait_ge(sig.index_ready[u][b], sig.index0[u] + sig.rounds + 1 - u)

            def experts(l):
                pairs(l, main[l])
                count = pool.value_load(more[0:1, 0:1], min_val=0, max_val=MORE_BLOCKS - 1)
                with pool.If(count > 0):
                    pairs(l, rest[l])

            link(pool.memset(ident[:, :], 0.0))
            pool.affine_select(out=ident[:, :], in_=ident[:, :], compare_op=ALU.not_equal, fill=1.0, base=0,
                               pattern=[[-1, P]], channel_multiplier=1).then_inc(ident_set, 1)
            link(pool.memset(ones[:, :], 1.0))
            pool.affine_select(out=before[:, :], in_=ones[:, :], compare_op=ALU.is_gt, fill=0.0, base=0,
                               pattern=[[1, P]], channel_multiplier=-1).then_inc(ident_set, 1)
            link(pool.memset(minus_half[:, :], -0.5))
            pool.dma_start(wst, w_spatial[0].rearrange("h i j -> i h j")).then_inc(even_landed, 16)
            pool.dma_start(wpool, w_pool[0].rearrange("g c d -> c g d")).then_inc(even_landed, 16)
            pool.dma_start(bsp, b_spatial[0:1].partition_broadcast(P)).then_inc(even_landed, 16)
            pool.dma_start(lnvg, ln_v_g[0:1, :].partition_broadcast(P)).then_inc(rows_landed, 16)
            pool.dma_start(lnvb, ln_v_b[0:1, :].partition_broadcast(P)).then_inc(rows_landed, 16)
            pool.dma_start(pscale[:, :], pool_scale[0].rearrange("(g p) -> p g", p=P),
                           allow_slow_non_contiguous=True).then_inc(rows_landed, 16)
            load_biases(0)
            pool.wait_ge(even_landed, 48)
            pool.affine_select(out=wst, in_=wst, compare_op=ALU.is_ge, fill=0.0, base=0,
                               pattern=[[0, SG_HEADS], [-1, P]], channel_multiplier=1).then_inc(tril_set, 1)
            pool.dma_start(convw[:, :, :], conv_w[0].rearrange("(k p) w -> p k w", p=P)).then_inc(even_landed, 16)
            pool.dma_start(convb[:, :], conv_b[0].rearrange("(k p) -> p k", p=P), allow_slow_non_contiguous=True).then_inc(even_landed, 16)
            pool.iota(iota_e[:, :], [[1, EXPERTS]], base=0, channel_multiplier=0, allow_small_or_imprecise_dtypes=True)
            pool.iota(first_more[:, :], [[-1, EXPERTS]], base=EXPERTS - 1, channel_multiplier=0,
                      allow_small_or_imprecise_dtypes=True)
            pool.iota(number_a[:, :].rearrange("p (c t) -> p c t", c=2), [[1, 2], [2 * P, TT]], base=-INVALID,
                      channel_multiplier=2, allow_small_or_imprecise_dtypes=True)
            pool.iota(iota_s[:, :], [[1, SLOTS]], base=0, channel_multiplier=0, allow_small_or_imprecise_dtypes=True)
            link(pool.memset(upper[0:SLOTS, :], 0.0))
            link(pool.memset(upper[SLOTS:P, :], 1.0))
            load_router(0)
            pool.wait_ge(even_landed, 80)
            pool.engine_nop().then_inc(consts_set, 1)
            powers(TT)
            load_gb(0)
            for l in range(DEPTH):
                powers(TT)
                load_gb(3 * l + 1)
                powers(TT)
                load_gb(3 * l + 2)
                masks(l)
                dispatch(l)
                if l + 1 < DEPTH:
                    load_router(l + 1)
                    load_biases(l + 1)
                experts(l)
                powers(TT)
                if l + 1 < DEPTH:
                    load_gb(3 * l + 3)
            for t in range(TT):
                pool.wait_ge(x_ready, TT * (3 * DEPTH - 1) + t + 1)
                pool.dma_start(out[0, t * P:(t + 1) * P, :], xs[:, t, :]).then_inc(out_stored, 16)
            pool.wait_ge(out_stored, 16 * TT)


_INS = ["x", "mem", "w_in_even", "w_pool", "pool_scale", "ln_v_g", "ln_v_b", "w_spatial", "b_spatial",
        "w_out_even", "w_in_odd", "conv_w", "conv_b", "w_out_odd", "wq_x", "wk_x", "wv_x", "wo_x",
        "ln_g", "ln_b", "wr_group", "br_group", "wr_expert", "br_expert", "w1", "w3", "w2"]


def kernel(**inputs):
    import numpy as _np
    import concourse.bacc as _bacc
    from concourse import mybir as _mybir
    from concourse.bass_utils import run_bass_kernel_spmd as _run

    nc = _bacc.Bacc("TRN2", target_bir_lowering=False, num_devices=1)
    arrays, args = {}, []
    for name in _INS:
        a = _np.ascontiguousarray(inputs[name])
        arrays[f"in_{name}_dram"] = a
        args.append(nc.dram_tensor(f"in_{name}_dram", a.shape, _mybir.dt.from_np(a.dtype), kind="ExternalInput").ap())
    args.append(nc.dram_tensor("out_0_dram", (1, S, D), F32, kind="ExternalOutput").ap())
    trunk(nc, *args)
    r = _run(nc, [arrays], core_ids=[0])
    return r.results[0]["out_0_dram"]
```

```python
from contextlib import ExitStack

import concourse.bass as bass
from concourse import mybir

F32, F32R, I32 = mybir.dt.float32, mybir.dt.float32r, mybir.dt.int32
ALU, ACT, AX = mybir.AluOpType, mybir.ActivationFunctionType, mybir.AxisListType

P = 128
D = 1024
KD = D // P
S = 512
TT = S // P
MEM = 256
MT = MEM // P
HALF = 512
SG_HEADS = 4
HEADS, HEAD_DIM = 4, 256
WINDOWS = (2, 4, 8, 16)
PAD = max(WINDOWS)
GROUPS, PER_GROUP = 4, 8
EXPERTS = GROUPS * PER_GROUP
HID = 512
NROUTE = GROUPS + EXPERTS
DEPTH = 2
ALPHA = (2.0 * DEPTH) ** 0.25
LN_EPS = 1e-5
SCALE = HEAD_DIM ** -0.5

SLOTS = 64
PAIRS = EXPERTS // 2
MORE_BLOCKS = 2 * S // SLOTS
MORE_PAIRS = MORE_BLOCKS // 2
BLOCKS = EXPERTS + MORE_BLOCKS + 4
INVALID = 1 << 20
BIG = 1e30

RING = 6
RAW = 2
SPLIT_HALVES = 2
BANKS = 8
PAIR_TILES = 6
XG0, XG1, HA, HB, TA, YA, TB, YB = range(8)
TILE_LAST = (HA, HA, HB, HB, YA, YB)
TILE_SLOT = (4, 5, 2, 3, 1, 0)
AHEAD = ((1, 0, 0, 0, 0, 0), (1, 1, 0, 0, 0, 0))
ROWS_ORDER = ((0, 0), (1, 0), (0, 1), (1, 1), (2, 0), (3, 0), (2, 1), (3, 1))
AHEAD_OF_V = ((0,), (1, 2), (3,), ())
MEMT_AT = (0, 1)
O_BEFORE = {6: (0, 1), 7: (2, 3)}
WO_ORDER = ((0, 0), (1, 0), (0, 1), (1, 1), (2, 0), (2, 1), (3, 0), (3, 1))
ROUTE_FIRST, ROUTE_AT = (0, 1), (3, 0)


def schedule():
    jobs, stream = {}, []
    count = [0]

    def job(*name):
        jobs[name] = count[0]
        count[0] += 1
        return jobs[name]

    def tile(kind, what, l, c, *last):
        stream.append((kind, (what, l, c), jobs.get(last)))

    def proj_rows(l, what):
        for t, c in WO_ORDER if what == "wo" else ROWS_ORDER:
            if what == "wo" and (t, c) == ROUTE_AT:
                xt_jobs(3 * l + 2, ROUTE_FIRST)
                for r in ROUTE_FIRST:
                    job("route", l, r)
            if what == "mix" and l == 0 and (t, c) == MEMT_AT:
                for m in range(MT):
                    for g in range(2):
                        job("memt", m, g)
            job(what, l, t, c)
        for c in range(2):
            tile("split", what, l, c, what, l, TT - 1, c)

    def k_tile(l, c):
        for j in range(2):
            job("k", l, c, j)
        tile("whole" if l else "split", "k", l, c, "k", l, c, 1)

    def v_tile(l, c):
        for m in range(MT):
            job("v", l, c, m)
        tile("whole" if l else "split", "v", l, c, "v", l, c, MT - 1)

    def xt_jobs(site, ts):
        for t in ts:
            for g in range(2):
                job("xt", site, t, g)

    def first_pair(l, js):
        for j in js:
            tile("moe", "moe", l, j)

    for l in range(DEPTH):
        if l == 0:
            for what in ("gate_v", "pool_a", "gate_u"):
                for m in range(4):
                    if what == "gate_v":
                        xt_jobs(0, AHEAD_OF_V[m])
                    job(what, m)
                tile("split", what, l, 0, what, 3)
            job("wst")
            for g in range(4):
                job("pool_y", g)
            for h in range(SG_HEADS):
                job("spatial", h)
        else:
            for c in range(2):
                for what in ("cg", "z", "bg"):
                    for m in range(4):
                        job(what, c, m)
                    tile("split", what, l, c, what, c, 3)
        proj_rows(l, "mix")
        if l == 0:
            for c in range(2):
                k_tile(l, c)
            for c in range(2):
                v_tile(l, c)
        xt_jobs(3 * l + 1, range(TT))
        for c in range(2):
            for m in range(4):
                job("q", l, c, m)
            tile("split", "q", l, c, "q", l, c, 3)
        job("s", l, 0)
        job("s", l, 1)
        for j in range(8):
            if j + 2 < 8:
                job("s", l, j + 2)
            for n in O_BEFORE.get(j, ()):
                job("o", l, n)
            job("pt", l, j)
        for n in range(4, 8):
            job("o", l, n)
        proj_rows(l, "wo")
        xt_jobs(3 * l + 2, [2])
        job("route", l, 2)
        if l == 0:
            k_tile(1, 0)
        xt_jobs(3 * l + 2, [3])
        job("route", l, 3)
        if l == 0:
            k_tile(1, 1)
            first_pair(l, (0, 1))
        job("rank", l)
        if l == 0:
            v_tile(1, 0)
            first_pair(l, (2, 3))
        job("table", l)
        if l == 0:
            v_tile(1, 1)
            tile("ahead", "ahead", l, 0, "route", l, TT - 1)
            first_pair(l, (4, 5))
        else:
            first_pair(l, [4])
            tile("ahead", "ahead", l, 1, "o", l, KD - 1)
            first_pair(l, (5, 0, 1, 2, 3))
            tile("ahead", "ahead", l, 0, "route", l, TT - 1)
        jobs["moe", l] = count[0]
        tile("pairs", "moe", l, None)
        count[0] += BANKS * PAIRS
        for t in range(TT):
            for c in range(2):
                job("sum", l, t, c)
        if l + 1 < DEPTH:
            xt_jobs(3 * l + 3, range(TT))
    return jobs, stream


def place_tiles(jobs, stream):
    uses, release = [0] * RING, [None] * RING
    tile_slots, splits, moe_uses = {}, {}, {}
    raws = 0
    for kind, name, last in stream:
        if kind in ("split", "whole"):
            slot = raws % RAW
            raws += 1
            free = release[slot]
            if kind == "split":
                number = len(splits)
                splits[name] = (number, last)
                release[slot] = ("split", number)
                for n in range(2):
                    release[RAW + 2 * (number % 2) + n] = ("filled", last)
            else:
                release[slot] = ("filled", last)
        elif kind == "moe":
            l, j = name[1:]
            slot = TILE_SLOT[j]
            moe_uses.setdefault(l, {})[slot] = uses[slot]
            free = release[slot]
        elif kind == "ahead":
            tile_slots[name] = (None, None, ("filled", last))
            continue
        else:
            l = name[1]
            for j, slot in enumerate(TILE_SLOT):
                uses[slot] += PAIRS // (1 + AHEAD[l][j]) - 1
                release[slot] = ("filled", jobs["moe", l] + BANKS * (PAIRS - 1 - AHEAD[l][j]) + TILE_LAST[j])
            continue
        uses[slot] += 1
        tile_slots[name] = (slot, uses[slot], free)
    return tile_slots, splits, moe_uses


def count_highs():
    done, total = {}, 0
    for l in range(DEPTH):
        for step, n in ((("xt", 3 * l), 2 * TT), (("mix", l), TT if l else KD), (("mem", l), 0 if l else 1),
                        (("xt", 3 * l + 1), 2 * TT), (("o", l), KD)):
            total += n
            done[step] = total
    return done


class Signals:

    def __init__(self, landed, filled, drained, gathered, silu, index_ready, stored, pool_step,
                 job0, slot_uses, ahead, runs, pair0, pairs):
        self.landed, self.filled, self.drained = landed, filled, drained
        self.gathered, self.silu, self.index_ready, self.stored = gathered, silu, index_ready, stored
        self.pool_step = pool_step
        self.ahead = ahead
        self.job0, self.slot_uses, self.pair0, self.pairs = job0, slot_uses, pair0, pairs
        self.rounds = pairs // 2
        self.ahead0 = (self.rounds * runs, 0)
        self.gathered0 = (self.rounds + 1) * runs
        self.silu0 = 2 * pairs * runs
        self.index0 = ((self.rounds + 1) * runs, self.rounds * runs)
        self.stored0 = self.rounds * runs
        self.step0 = (pairs + 2) * runs

    def bank(self, j):
        return (self.job0 + j) % BANKS

    def wait_filled(self, eng, j, p, before=0):
        eng.wait_ge(self.filled[self.bank(j)], (self.job0 + j) // BANKS + 1 - before + p)

    def wait_drained(self, eng, j, p, before=0):
        eng.wait_ge(self.drained[self.bank(j)], (self.job0 + j) // BANKS + 1 - before + p)


def trunk(nc, x, mem, w_in_even, w_pool, pool_scale, ln_v_g, ln_v_b, w_spatial, b_spatial,
          w_out_even, w_in_odd, conv_w, conv_b, w_out_odd, wq_x, wk_x, wv_x, wo_x,
          ln_g, ln_b, wr_group, br_group, wr_expert, br_expert, w1, w3, w2, out):
    jobs, stream = schedule()
    tile_slots, splits, moe_uses = place_tiles(jobs, stream)
    highs_done = count_highs()

    with ExitStack() as ctx:
        def sb(name, shape, dt=F32):
            return ctx.enter_context(nc.sbuf_tensor(name, shape, dt))

        def sem(name):
            return ctx.enter_context(nc.semaphore(name))

        def parts(name, at_, chunks, width):
            return nc.alloc_sbuf_tensor_at(name, [P, chunks, width], F32R, offset=at_)

        def next_at():
            return (nc.sbuf_base + 31) // 32 * 32

        ring_at = next_at()
        ring = sb("ring", [P, RING, KD * HALF])
        xs = sb("xs", [P, TT, D])
        area_x_at = next_at()
        area_x = sb("area_x", [P, 4096])
        area_a_at = next_at()
        area_a = sb("area_a", [P, 4096])
        area_b_at = next_at()
        area_b = sb("area_b", [P, 4160])
        slot_bytes = 4 * KD * HALF
        w_hi = [parts(f"w_hi{n}", ring_at + (RAW + 2 * n) * slot_bytes, KD, HALF) for n in range(2)]
        w_lo = [parts(f"w_lo{n}", ring_at + (RAW + 2 * n + 1) * slot_bytes, KD, HALF) for n in range(2)]
        mem_hi = parts("mem_hi", area_b_at, KD, MEM)
        mem_lo = parts("mem_lo", area_b_at + 4 * KD * MEM, KD, MEM)
        x_hi, x_lo = parts("x_hi", area_x_at, KD, S), parts("x_lo", area_a_at, KD, S)
        o_hi, o_lo = parts("o_hi", area_a_at, KD, S), parts("o_lo", area_b_at, KD, S)
        area_kv = sb("area_kv", [P, 4096])
        area_e = sb("area_e", [P, 2560])
        work = sb("work", [P, 2, D])
        gb = sb("gb", [P, 2, D])
        ident = sb("ident", [P, P])
        ones = sb("ones", [P, P])
        before = sb("before", [P, P])
        wr = sb("wr", [P, KD, NROUTE])
        br = sb("br", [P, NROUTE])
        stats = sb("stats", [P, 12])
        mean_var = [sb(f"mean_var{n}", [P, 2]) for n in range(2)]
        var_eps = [sb(f"var_eps{n}", [P, 1]) for n in range(2)]
        rstd = [sb(f"rstd{n}", [P, 1]) for n in range(2)]
        minus_half = sb("minus_half", [P, 1])
        pscale = sb("pscale", [P, 4])
        inv_count = sb("inv_count", [P, PAD])
        convw = sb("convw", [P, KD, 3])
        convb = sb("convb", [P, KD])
        smax = sb("smax", [P, 2, 2])
        nsmax = sb("nsmax", [P, 2, 2])
        ssum = sb("ssum", [P, 2, 2])
        srec = sb("srec", [P, 2, 2])
        iota_e = sb("iota_e", [P, EXPERTS])
        first_more = sb("first_more", [P, EXPERTS])
        iota_s = sb("iota_s", [P, SLOTS])
        number_a = sb("number_a", [P, 2 * TT])
        place = sb("place", [P, 2 * TT], I32)
        place_lo = sb("place_lo", [P, 2 * TT], I32)
        gates = sb("gates", [P, TT, 2])
        raw = sb("raw", [P, BLOCKS], I32)
        to_row = sb("to_row", [P, BLOCKS], I32)
        from_row = sb("from_row", [P, BLOCKS // 2], I32)
        upper = sb("upper", [P, 1])
        gather_index = [sb(f"gather_index{u}", [P, 1], I32) for u in range(2)]
        store_index = [[sb(f"store_index{u}{b}", [P, 1], I32) for b in "ab"] for u in range(2)]
        more = sb("more", [P, 1 + MORE_BLOCKS], I32)
        ps = ctx.enter_context(nc.psum_tensor("ps", [P, BANKS, HALF], F32))

        tile_ahead = [area[:, :].rearrange("p (k n) -> p k n", k=KD) for area in (area_x, area_kv)]
        xt = area_x[:, :].rearrange("p (k s) -> p k s", k=KD)
        mixt = area_b[:, 0:4096].rearrange("p (k s) -> p k s", k=KD)
        qt = mixt
        at = area_b[:, 0:4 * (PAD + S)].rearrange("p (g s) -> p g s", g=4)
        ut = area_b[:, 4 * (PAD + S):4 * (PAD + S) + 4 * S].rearrange("p (g s) -> p g s", g=4)
        gate_rows = work[:, :, :].rearrange("p a (m s) -> p (a m) s", m=2)
        cgt = work[:, :, :].rearrange("p a (m s) -> p (a m) s", m=2)
        zct = area_e[:, 0:4 * (S + 2)].rearrange("p (m s) -> p m s", m=4)
        pt = area_x[:, :].rearrange("p (h m s) -> p h m s", h=HEADS, m=MT)
        vn = area_kv[:, 0:2048].rearrange("p (t c) -> p t c", t=TT)
        dt_ = area_kv[:, 2048:4096].rearrange("p (g s) -> p g s", g=4)
        kt = area_kv[:, 0:2048].rearrange("p (n m) -> p n m", n=KD)
        va = area_kv[:, 2048:4096].rearrange("p (m d) -> p m d", m=MT)
        wpool = area_e[:, 0:512].rearrange("p (g d) -> p g d", g=4)
        wst = area_e[:, 512:1024].rearrange("p (h i) -> p h i", h=SG_HEADS)
        bsp = area_e[:, 1024:1536].rearrange("p (h i) -> p h i", h=SG_HEADS)
        lnvg, lnvb = area_e[:, 1536:2048], area_e[:, 2048:2560]
        mem_rows = gb
        memt = area_e[:, 0:2048].rearrange("p (k m) -> p k m", k=KD)
        more_x = area_b[:, 3072:3072 + MORE_BLOCKS * EXPERTS].rearrange("p (a b) -> p a b", a=MORE_BLOCKS)
        flat = work[:, :, :].rearrange("p a b -> p (a b)")
        used = [0]

        def small(n):
            used[0] += n
            assert used[0] <= 2 * D
            return flat[:, used[0] - n:used[0]]

        logits = area_e[:, 2064:2064 + TT * NROUTE].rearrange("p (t n) -> p t n", t=TT)
        oh_g = small(TT * GROUPS).rearrange("p (t g) -> p t g", t=TT)
        cand_g = small(TT * GROUPS).rearrange("p (t g) -> p t g", t=TT)
        exp_g = small(TT * GROUPS).rearrange("p (t g) -> p t g", t=TT)
        lm = small(TT * EXPERTS).rearrange("p (t e) -> p t e", t=TT)
        cand = small(TT * EXPERTS).rearrange("p (t e) -> p t e", t=TT)
        oh = [small(TT * EXPERTS).rearrange("p (t e) -> p t e", t=TT) for _ in range(2)]
        chosen = small((TT + 1) * EXPERTS)
        rank_i = small(TT * EXPERTS).bitcast(I32).rearrange("p (t e) -> p t e", t=TT)
        rank_hi = small(TT * EXPERTS).bitcast(I32).rearrange("p (t e) -> p t e", t=TT)
        slot = small(TT * EXPERTS).rearrange("p (t e) -> p t e", t=TT)
        gmax, gmin, v0, v1, gsum, dexp, scr = (small(TT) for _ in range(7))
        extra_i = small(EXPERTS).bitcast(I32)
        scan = [small(EXPERTS // 2 + EXPERTS) for _ in range(2)]
        upto_n, below_n = (scan[1][:, EXPERTS // 2 - n:EXPERTS // 2 - n + EXPERTS] for n in range(2))
        base_n = small(EXPERTS)
        place_n = small(2 * TT)
        more_n = small(MORE_BLOCKS)
        diag = flat[:, 0:(2 * TT + 1) * P].rearrange("p (n s) -> p n s", n=2 * TT + 1)
        at_slot = area_a[:, 0:2 * TT * P].rearrange("p (n s) -> p n s", n=2 * TT)
        at_block = area_a[:, 2 * TT * P:2 * TT * (P + BLOCKS)].rearrange("p (n b) -> p n b", n=2 * TT)
        xg = [area_b[:, 0:1024], area_b[:, 2048:3072]]
        xgt = area_b[:, 1024:2048].rearrange("p (k s) -> p k s", k=KD)
        silu_sb = [area_a[0:SLOTS, 512 * b:512 * b + 512] for b in range(2)]
        hid = [area_a[0:SLOTS, 1024 + 512 * b:1536 + 512 * b] for b in range(2)]
        hidt = [area_a[:, 2048 + 256 * b:2304 + 256 * b].rearrange("p (j s) -> p j s", j=4) for b in range(2)]
        ysb = [[area_a[:, 2560 + 512 * b:3072 + 512 * b] for b in range(2)],
               [area_b[:, 3072 + 512 * b:3584 + 512 * b] for b in range(2)]]
        y_pair = [area_b[:, 0:2048], area_b[:, 2048:4096]]
        y_slot = RAW + 2 * ((splits["cg", 1, 0][0] + 1) % 2)
        y_pair += [ring[:, y_slot, 0:2 * D], ring[:, y_slot, 2 * D:4 * D]]

        x_dram = [nc.dram_tensor(f"x_rows{l}", [S, D], F32, kind="Internal").ap() for l in range(DEPTH)]
        y_dram = [nc.dram_tensor(f"y_rows{l}", [4 * S, HALF], F32, kind="Internal").ap() for l in range(DEPTH)]

        landed = [sem(f"slot_landed{n}") for n in range(RING)]
        filled = [sem(f"bank_filled{n}") for n in range(BANKS)]
        drained = [sem(f"bank_drained{n}") for n in range(BANKS)]
        w_hi_set = sem("w_hi_set")
        w_lo_set = sem("w_lo_set")
        hi_set = sem("hi_set")
        mem_landed = sem("mem_landed")
        half_landed = sem("half_landed")
        mem_lo_set = sem("mem_lo_set")
        ahead_landed = [sem(f"ahead_landed{j}") for j in range(2)]
        x_landed = [sem(f"x_landed{n}") for n in range(TT)]
        even_landed = sem("even_landed")
        rows_landed = sem("rows_landed")
        gb_landed = sem("gb_landed")
        router_landed = sem("router_landed")
        ident_set = sem("ident_set")
        pool_set = sem("pool_set")
        consts_set = sem("consts_set")
        tril_set = sem("tril_set")
        dve_step = sem("dve_step")
        var_ready = sem("var_ready")
        rstd_ready = sem("rstd_ready")
        x_ready = sem("x_ready")
        vn_ready = sem("vn_ready")
        pooled = sem("pooled")
        smax_ready = sem("smax_ready")
        p_ready = sem("p_ready")
        gated = sem("gated")
        mixt_ready = sem("mixt_ready")
        chosen_ready = sem("chosen_ready")
        place_ready = sem("place_ready")
        gate_in_ready = sem("gate_in_ready")
        gate_exp_ready = sem("gate_exp_ready")
        rows_known = sem("rows_known")
        more_known = sem("more_known")
        xg_cleared = sem("xg_cleared")
        x_stored = sem("x_stored")
        y_landed = [[sem(f"y_landed{t}{e}") for e in range(2)] for t in range(TT)]
        diag_set = sem("diag_set")
        row_centred = sem("row_centred")
        out_stored = sem("out_stored")
        pool_step = sem("pool_step")
        index_seen = sem("index_seen")
        gathered = [sem(f"gathered{u}") for u in range(2)]
        silu_done = sem("silu_done")
        index_ready = [[sem(f"index_ready{u}{b}") for b in "ab"] for u in range(2)]
        stored = [[sem(f"stored{u}{b}") for b in "ab"] for u in range(2)]

        main, rest = [], []
        for l in range(DEPTH):
            main.append(Signals(landed, filled, drained, gathered, silu_done, index_ready, stored, pool_step,
                                jobs["moe", l], moe_uses[l], AHEAD[l], l, 0, PAIRS))
            m = f"more{l}"
            rest.append(Signals([sem(f"{m}_landed{n}") for n in range(RING)],
                                [sem(f"{m}_filled{n}") for n in range(BANKS)],
                                [sem(f"{m}_drained{n}") for n in range(BANKS)],
                                [sem(f"{m}_gathered{u}") for u in range(2)], sem(f"{m}_silu"),
                                [[sem(f"{m}_index{u}{b}") for b in "ab"] for u in range(2)],
                                [[sem(f"{m}_stored{u}{b}") for b in "ab"] for u in range(2)],
                                sem(f"{m}_step"), BANKS, [0] * RING, (0,) * PAIR_TILES, 0, PAIRS, MORE_PAIRS))

        def wait_filled(eng, *name):
            eng.wait_ge(filled[jobs[name] % BANKS], jobs[name] // BANKS + 1)

        def wait_drained(eng, *name):
            eng.wait_ge(drained[jobs[name] % BANKS], jobs[name] // BANKS + 1)

        def bank(*name):
            return ps[:, jobs[name] % BANKS, :]

        def is_drained(*name):
            return drained[jobs[name] % BANKS], 1

        def tile_view(slot, k):
            return ring[:, slot, 0:k * (KD * HALF // k)].rearrange("p (k n) -> p k n", k=k)

        split_chunks = KD // SPLIT_HALVES

        def split_number(what, l, c):
            return splits[what, l, c][0]

        def wait_pair_free(eng, number):
            if number >= 2:
                last = next(j for n, j in splits.values() if n == number - 2)
                eng.wait_ge(filled[last % BANKS], last // BANKS + 1)

        block = ctx.enter_context(nc.Block())

        @block.sync
        def _(sp):
            def halves(w, cols):
                return w.rearrange("(k p) n -> p k n", p=P)[:, :, cols]

            def cut(c):
                return slice(c * HALF, (c + 1) * HALF)

            source = {}
            for c, what in enumerate(("pool_a", "gate_u", "gate_v")):
                source[what, 0, 0] = halves(w_in_even[0], cut(c))
            for c in range(2):
                source["mix", 0, c] = halves(w_out_even[0], cut(c))
                source["mix", 1, c] = halves(w_out_odd[0], cut(c))
                for n, what in enumerate(("bg", "cg", "z")):
                    source[what, 1, c] = halves(w_in_odd[0], cut(2 * n + c))
                for l in range(DEPTH):
                    for what, w in (("q", wq_x), ("k", wk_x), ("v", wv_x), ("wo", wo_x)):
                        source[what, l, c] = halves(w[l], cut(c))

            def wait_free(free):
                if free and free[0] == "filled":
                    sp.wait_ge(filled[free[1] % BANKS], free[1] // BANKS + 1)
                elif free:
                    sp.wait_ge(w_lo_set, SPLIT_HALVES * (free[1] + 1))

            def expert_rows(w, l, e, k):
                return w[l, bass.ds(e, 1)].rearrange("o (p k) n -> p (o k) n", k=k)

            def load_expert(l, sig, j, blocks, apart=False):
                a, b = blocks
                w, e, k = ((w1, a, 8), (w3, a, 8), (w1, b, 8), (w3, b, 8), (w2, a, 4), (w2, b, 4))[j]
                slot = TILE_SLOT[j]
                place_, signal = (tile_ahead[j], ahead_landed[j]) if apart else (tile_view(slot, k), sig.landed[slot])
                sp.dma_start(place_, expert_rows(w, l, e, k)).then_inc(signal, 16)

            def load_pair(l, sig, p, blocks, js=range(PAIR_TILES), apart=False):
                for j in js:
                    sig.wait_filled(sp, TILE_LAST[j], p, before=1)
                    load_expert(l, sig, j, blocks, apart)

            def wait_stored(sig):
                for u in range(2):
                    for b in range(2):
                        sp.wait_ge(sig.stored[u][b], 16 * (sig.stored0 + sig.rounds))

            def load_outputs(l):
                wait_stored(main[l])
                rows_of = y_dram[l].rearrange("(t p r) n -> t p (r n)", p=P, r=4)
                for t in range(TT):
                    for e in range(2):
                        cols = slice(e * D, (e + 1) * D)
                        sp.dma_start(y_pair[t][:, cols], rows_of[t][:, cols]).then_inc(y_landed[t][e], 16)

            def load_x(t):
                sp.dma_start(xs[:, t, :], x[0, t * P:(t + 1) * P, :]).then_inc(x_landed[t], 16)
            for n, (kind, name, _) in enumerate(stream):
                l = name[1]
                if n == 0:
                    load_x(0)
                    for half, signal in enumerate((half_landed, landed[tile_slots[name][0]])):
                        ks = slice(half * split_chunks, (half + 1) * split_chunks)
                        sp.dma_start(tile_view(tile_slots[name][0], KD)[:, ks, :], source[name][:, ks, :]).then_inc(signal, 16)
                    for t in range(1, TT):
                        load_x(t)
                    continue
                if n == 2:
                    sp.dma_start(mem_rows[:, :, :], mem[0].rearrange("(m p) d -> p m d", p=P)).then_inc(mem_landed, 16)
                if kind in ("split", "whole"):
                    slot, _, free = tile_slots[name]
                    wait_free(free)
                    sp.dma_start(tile_view(slot, KD), source[name]).then_inc(landed[slot], 16)
                    if name == ("cg", 1, 0):
                        load_outputs(0)
                elif kind == "moe":
                    wait_free(tile_slots[name][2])
                    load_expert(l, main[l], name[2], (0, 1))
                elif kind == "ahead":
                    wait_free(tile_slots[name][2])
                    load_expert(l, main[l], name[2], (2, 3), apart=True)
                else:
                    early = [j for j in range(PAIR_TILES) if AHEAD[l][j]]
                    others = [j for j in range(PAIR_TILES) if not AHEAD[l][j]]
                    with sp.Fori(1, PAIRS // 2) as i:
                        for u in range(2):
                            p = 2 * i + (u - 1)
                            load_pair(l, main[l], p, (4 * i + 2 * u, 4 * i + (2 * u + 1)), early, apart=(u == 1))
                            load_pair(l, main[l], p, (4 * i + (2 * u - 2), 4 * i + (2 * u - 1)), others)
                    load_pair(l, main[l], PAIRS - 1, (2 * PAIRS - 2, 2 * PAIRS - 1), others)
                    sp.wait_ge(more_known, l + 1)
                    count = sp.value_load(more[0:1, 0:1], min_val=0, max_val=MORE_BLOCKS - 1)
                    with sp.If(count > 0):
                        with sp.Fori(0, MORE_PAIRS) as i:
                            a = sp.value_load(more[0:1, bass.ds(2 * i + 1, 1)], min_val=0, max_val=EXPERTS - 1)
                            b = sp.value_load(more[0:1, bass.ds(2 * i + 2, 1)], min_val=0, max_val=EXPERTS - 1)
                            load_pair(l, rest[l], i, (a, b))
                        for j in set(TILE_LAST):
                            rest[l].wait_filled(sp, j, MORE_PAIRS - 1)
                        wait_stored(rest[l])
                    if l + 1 == DEPTH:
                        load_outputs(l)
            for t in range(TT):
                sp.wait_ge(x_ready, TT * (3 * DEPTH - 1) + t + 1)
                sp.dma_start(out[0, t * P:(t + 1) * P, :], xs[:, t, :]).then_inc(out_stored, 16)
            sp.wait_ge(out_stored, 16 * TT)

        @block.tensor
        def _(pe):
            order = [0]

            def begin(*name):
                n = jobs[name]
                assert n == order[0], name
                order[0] += 1
                if n >= BANKS:
                    pe.wait_ge(drained[n % BANKS], n // BANKS)
                return ps[:, n % BANKS, :], filled[n % BANKS]

            def weights(what, l, c):
                slot, uses, _ = tile_slots[what, l, c]
                pe.wait_ge(landed[slot], 16 * uses)
                return tile_view(slot, KD)

            known = set()

            def split_product(dst, tile, x_known, operands, w_low_last=False):
                number = split_number(*tile)
                passes = ((0, 0), (1, 0), (0, 1)) if w_low_last else ((0, 0), (0, 1), (1, 0))
                for n, (x_low, w_low) in enumerate(passes):
                    if n == 0 or x_low:
                        x_known(x_low)
                    for k in range(KD):
                        if k % split_chunks == 0 and not x_low and (number, w_low, k) not in known:
                            known.add((number, w_low, k))
                            pe.wait_ge(w_lo_set if w_low else w_hi_set, SPLIT_HALVES * number + k // split_chunks + 1)
                        stationary, moving = operands(k, x_low, w_low)
                        mm = pe.matmul(dst, stationary, moving, start=(n == 0 and k == 0),
                                       stop=(n == 2 and k == KD - 1))
                return mm

            def columns(name, tile, m, x_known):
                turn = split_number(*tile) % 2
                dst, done = begin(*name)
                split_product(dst, tile, x_known, lambda k, x_low, w_low: (
                    (w_hi, w_lo)[w_low][turn][:, k, m * P:(m + 1) * P], (x_hi, x_lo)[x_low][:, k, :])).then_inc(done, 1)

            def rows(name, tile, parts_, t, x_known, w_low_last=False):
                turn = split_number(*tile) % 2
                dst, done = begin(*name)
                split_product(dst, tile, x_known, lambda k, x_low, w_low: (
                    parts_[x_low][:, k, t * P:(t + 1) * P], (w_hi, w_lo)[w_low][turn][:, k, :]), w_low_last)\
                    .then_inc(done, 1)

            def mem_known(low):
                if ("mem", low) not in known:
                    known.add(("mem", low))
                    pe.wait_ge(mem_lo_set if low else hi_set, 1 if low else highs_done["mem", 0])

            def xt_known(site, ts=range(TT)):
                def wait(low):
                    if ("xt", site, low, ts[-1]) in known:
                        return
                    known.add(("xt", site, low, ts[-1]))
                    if not low:
                        pe.wait_ge(hi_set, highs_done["xt", site] - 2 * (TT - 1 - ts[-1]))
                    else:
                        for t in ts:
                            for g in range(2):
                                wait_drained(pe, "xt", site, t, g)
                return wait

            def transposes(name, pieces):
                dst, done = begin(*name)
                for q, piece in enumerate(pieces):
                    mm = pe.transpose(dst[:, q * P:(q + 1) * P], piece, ident[:, :])
                mm.then_inc(done, 1)

            def transpose_x(site, ts):
                for t in ts:
                    if site:
                        pe.wait_ge(x_ready, TT * (site - 1) + t + 1)
                    else:
                        pe.wait_ge(x_landed[t], 16)
                    for g in range(2):
                        transposes(("xt", site, t, g), [xs[:, t, (4 * g + q) * P:(4 * g + q + 1) * P] for q in range(4)])

            def wait_xt(site, ts=range(TT)):
                for t in ts:
                    for g in range(2):
                        wait_drained(pe, "xt", site, t, g)

            def transpose_mem():
                pe.wait_ge(mem_landed, 16)
                for m in range(MT):
                    for g in range(2):
                        transposes(("memt", m, g), [mem_rows[:, m, (4 * g + q) * P:(4 * g + q + 1) * P] for q in range(4)])

            def rows_both(l, what, parts_, x_known):
                for t, c in WO_ORDER if what == "wo" else ROWS_ORDER:
                    if what == "wo" and (t, c) == ROUTE_AT:
                        transpose_x(3 * l + 2, ROUTE_FIRST)
                        for r in ROUTE_FIRST:
                            route(l, r)
                    if what == "mix" and l == 0 and (t, c) == MEMT_AT:
                        transpose_mem()
                    rows((what, l, t, c), (what, l, c), parts_, t, lambda low: x_known(low, t, c))

            def split_keys(c):
                turn = split_number("k", 0, c) % 2
                for j in range(2):
                    dst, done = begin("k", 0, c, j)
                    for m in range(2):
                        cols = slice((2 * j + m) * P, (2 * j + m + 1) * P)
                        mm = split_product(dst[:, m * MEM:(m + 1) * MEM], ("k", 0, c), mem_known, lambda k, x_low, w_low: (
                            (w_hi, w_lo)[w_low][turn][:, k, cols], (mem_hi, mem_lo)[x_low][:, k, :]))
                    mm.then_inc(done, 1)

            def split_values(c):
                for m in range(MT):
                    rows(("v", 0, c, m), ("v", 0, c), (mem_hi, mem_lo), m, mem_known)

            def keys(l, c):
                w = weights("k", l, c)
                for j in range(2):
                    dst, done = begin("k", l, c, j)
                    for m in range(2):
                        n = 2 * j + m
                        for k in range(KD):
                            mm = pe.matmul(dst[:, m * MEM:(m + 1) * MEM], w[:, k, n * P:(n + 1) * P], memt[:, k, :],
                                           start=(k == 0), stop=(k == KD - 1))
                    mm.then_inc(done, 1)

            def values(l, c):
                w = weights("v", l, c)
                for m in range(MT):
                    dst, done = begin("v", l, c, m)
                    for k in range(KD):
                        mm = pe.matmul(dst, memt[:, k, m * P:(m + 1) * P], w[:, k, :], start=(k == 0), stop=(k == KD - 1))
                    mm.then_inc(done, 1)

            def even_mixer():
                for t in range(TT):
                    transpose_x(0, AHEAD_OF_V[t])
                    rows(("gate_v", t), ("gate_v", 0, 0), (x_hi, x_lo), t, xt_known(0, [t]), w_low_last=True)
                for what in ("pool_a", "gate_u"):
                    for m in range(4):
                        columns((what, m), (what, 0, 0), m, xt_known(0))
                pe.wait_ge(tril_set, 1)
                transposes(("wst",), [wst[:, h, :] for h in range(SG_HEADS)])
                for g in range(4):
                    pe.wait_ge(pooled, g + 1)
                    dst, done = begin("pool_y", g)
                    pe.matmul(dst, wpool[:, g, :], dt_[:, g, :], start=True, stop=True).then_inc(done, 1)
                pe.wait_ge(vn_ready, TT)
                wait_drained(pe, "wst")
                for h in range(SG_HEADS):
                    dst, done = begin("spatial", h)
                    for t in range(TT):
                        mm = pe.matmul(dst[:, t * P:(t + 1) * P], vn[:, t, h * P:(h + 1) * P], wst[:, h, :],
                                       start=True, stop=True)
                    mm.then_inc(done, 1)

                def mixed(low, t, c):
                    if (t, c) != ROWS_ORDER[0]:
                        return
                    if not low:
                        pe.wait_ge(hi_set, highs_done["mix", 0])
                    else:
                        for g in range(4):
                            wait_drained(pe, "pool_y", g)
                        pe.wait_ge(mixt_ready, SG_HEADS)
                rows_both(0, "mix", (x_hi, x_lo), mixed)

            def odd_mixer():
                for c in range(2):
                    for what in ("cg", "z", "bg"):
                        for m in range(4):
                            columns((what, c, m), (what, 1, c), m, xt_known(3))

                def mixed(low, t, c):
                    if c == 0:
                        if not low:
                            pe.wait_ge(hi_set, highs_done["xt", 3] + t + 1)
                        else:
                            pe.wait_ge(mixt_ready, SG_HEADS + t + 1)
                rows_both(1, "mix", (x_hi, x_lo), mixed)

            def scores(l, j):
                t, hp = j % TT, j // TT
                dst, done = begin("s", l, j)
                for h in range(2):
                    for k in range(2):
                        n = 2 * (2 * hp + h) + k
                        mm = pe.matmul(dst[:, h * MEM:(h + 1) * MEM], qt[:, n, t * P:(t + 1) * P], kt[:, n, :],
                                       start=(k == 0), stop=(k == 1))
                mm.then_inc(done, 1)

            def attention(l):
                for c in range(2):
                    for m in range(4):
                        columns(("q", l, c, m), ("q", l, c), m, xt_known(3 * l + 1))
                for c in range(2):
                    for j in range(2):
                        wait_drained(pe, "k", l, c, j)
                    for m in range(4):
                        wait_drained(pe, "q", l, c, m)
                scores(l, 0)
                scores(l, 1)
                def outputs(ns):
                    for n in ns:
                        if n in (0, 4):
                            for j in range(n, n + 4):
                                wait_drained(pe, "pt", l, j)
                        dst, done = begin("o", l, n)
                        for m in range(MT):
                            mm = pe.matmul(dst, va[:, m, n * P:(n + 1) * P], pt[:, n // 2, m, :],
                                           start=(m == 0), stop=(m == MT - 1))
                        mm.then_inc(done, 1)

                for j in range(8):
                    if j + 2 < 8:
                        scores(l, j + 2)
                    if j in O_BEFORE and O_BEFORE[j][0] == 0:
                        for c in range(2):
                            for m in range(MT):
                                wait_drained(pe, "v", l, c, m)
                    outputs(O_BEFORE.get(j, ()))
                    pe.wait_ge(p_ready, 8 * l + j + 1)
                    transposes(("pt", l, j), [work[:, j % 2, q * P:(q + 1) * P] for q in range(4)])
                outputs(range(4, 8))

                def mixed(low, t, c):
                    if (t, c) != ROWS_ORDER[0]:
                        return
                    if not low:
                        pe.wait_ge(hi_set, highs_done["o", l])
                    else:
                        for n in range(8):
                            wait_drained(pe, "o", l, n)
                rows_both(l, "wo", (o_hi, o_lo), mixed)

            def route(l, t):
                wait_xt(3 * l + 2, [t])
                pe.wait_ge(router_landed, 16 * 5 * (l + 1))
                dst, done = begin("route", l, t)
                for k in range(KD):
                    mm = pe.matmul(dst[:, 0:NROUTE], xt[:, k, t * P:(t + 1) * P], wr[:, k, :],
                                   start=(k == 0), stop=(k == KD - 1))
                mm.then_inc(done, 1)

            def rank(l):
                pe.wait_ge(chosen_ready, l + 1)
                dst, done = begin("rank", l)
                width = (TT + 1) * EXPERTS
                pe.matmul(dst[:, 0:width], before[:, :], chosen, start=True, stop=False)
                for b in range(1, TT + 1):
                    mm = pe.matmul(dst[:, b * EXPERTS:width], ones[:, :], chosen[:, 0:width - b * EXPERTS],
                                   start=False, stop=(b == TT))
                mm.then_inc(done, 1)

            def slot_table(l):
                pe.wait_ge(place_ready, l + 1)
                dst, done = begin("table", l)
                for n in range(2 * TT):
                    mm = pe.matmul(dst[:, 0:BLOCKS], at_slot[:, n, :], at_block[:, n, :],
                                   start=(n == 0), stop=(n == 2 * TT - 1))
                mm.then_inc(done, 1)

            def pair(sig, u, i):
                p = 2 * i + u

                def tile(j, k):
                    slot = TILE_SLOT[j]
                    if sig.ahead[j] and u == 1:
                        pe.wait_ge(ahead_landed[j], 16 * (sig.ahead0[j] + 1 + i))
                        return tile_ahead[j]
                    pe.wait_ge(sig.landed[slot], 16 * (sig.slot_uses[slot] + 1 + (i if sig.ahead[j] else p)))
                    return tile_view(slot, k)

                def bank_of(j):
                    sig.wait_drained(pe, j, p, before=1)
                    return ps[:, sig.bank(j), :]

                pe.wait_ge(sig.gathered[u], 16 * (sig.gathered0 + 1 + i))
                for j in (XG0, XG1):
                    dst = bank_of(j)
                    for q in range(4):
                        k = 4 * (j - XG0) + q
                        mm = pe.transpose(dst[:, q * P:(q + 1) * P], xg[u][:, k:D:KD], ident[:, :])
                    mm.then_inc(sig.filled[sig.bank(j)], 1)
                sig.wait_drained(pe, XG0, p)
                sig.wait_drained(pe, XG1, p)
                for b, j in enumerate((HA, HB)):
                    ws = [tile(2 * b, 8), tile(2 * b + 1, 8)]
                    dst = bank_of(j)
                    for k in range(KD):
                        for half in range(2):
                            mm = pe.matmul(dst[half * SLOTS:(half + 1) * SLOTS, :],
                                           xgt[:, k, b * SLOTS:(b + 1) * SLOTS], ws[half][:, k, :],
                                           start=(k == 0), stop=(k == KD - 1))
                    mm.then_inc(sig.filled[sig.bank(j)], 1)
                for b, (jh, jt, jy) in enumerate(((HA, TA, YA), (HB, TB, YB))):
                    pe.wait_ge(ident_set, 2)
                    sig.wait_drained(pe, jh, p)
                    dst = bank_of(jt)
                    for q in range(4):
                        mm = pe.transpose(dst[:, q * SLOTS:(q + 1) * SLOTS], hid[b][:, q * P:(q + 1) * P],
                                          ident[0:SLOTS, 0:SLOTS])
                    mm.then_inc(sig.filled[sig.bank(jt)], 1)
                    w = tile(4 + b, 4)
                    sig.wait_drained(pe, jt, p)
                    dst = bank_of(jy)
                    for q in range(4):
                        for half in range(2):
                            mm = pe.matmul(dst[half * SLOTS:(half + 1) * SLOTS, :], hidt[b][:, q, :],
                                           w[:, q, half * HALF:(half + 1) * HALF], start=(q == 0), stop=(q == 3))
                    mm.then_inc(sig.filled[sig.bank(jy)], 1)

            def experts(l):
                with pe.Fori(0, main[l].rounds) as i:
                    for u in range(2):
                        pair(main[l], u, i)
                order[0] += BANKS * PAIRS
                pe.wait_ge(more_known, l + 1)
                count = pe.value_load(more[0:1, 0:1], min_val=0, max_val=MORE_BLOCKS - 1)
                with pe.If(count > 0):
                    for j in range(BANKS):
                        main[l].wait_drained(pe, j, PAIRS - 1)
                    for n in range(BANKS):
                        pe.sem_inc(rest[l].filled[n], 1)
                        pe.sem_inc(rest[l].drained[n], 1)
                    with pe.Fori(0, rest[l].rounds) as i:
                        for u in range(2):
                            pair(rest[l], u, i)
                    for j in range(BANKS):
                        rest[l].wait_drained(pe, j, MORE_PAIRS - 1)

            def sums(l):
                pe.wait_ge(diag_set, l + 1)
                for t in range(TT):
                    for c in range(2):
                        dst, _ = begin("sum", l, t, c)
                        pe.matmul(dst, diag[:, 2 * TT, :], xs[:, t, c * HALF:(c + 1) * HALF], start=True, stop=False)
                for t in range(TT):
                    for e in range(2):
                        pe.wait_ge(y_landed[t][e], 16 * (l + 1))
                        for c in range(2):
                            n = jobs["sum", l, t, c] % BANKS
                            mm = pe.matmul(ps[:, n, :], diag[:, 2 * t + e, :],
                                           y_pair[t][:, e * D + c * HALF:e * D + (c + 1) * HALF], start=False, stop=(e == 1))
                            if e:
                                mm.then_inc(filled[n], 1)

            pe.wait_ge(ident_set, 2)
            for l in range(DEPTH):
                if l == 0:
                    even_mixer()
                else:
                    odd_mixer()
                if l == 0:
                    for c in range(2):
                        split_keys(c)
                    for c in range(2):
                        split_values(c)
                transpose_x(3 * l + 1, range(TT))
                attention(l)
                transpose_x(3 * l + 2, [2])
                route(l, 2)
                if l == 0:
                    keys(1, 0)
                transpose_x(3 * l + 2, [3])
                route(l, 3)
                if l == 0:
                    keys(1, 1)
                rank(l)
                if l == 0:
                    values(1, 0)
                slot_table(l)
                if l == 0:
                    values(1, 1)
                experts(l)
                sums(l)
                if l + 1 < DEPTH:
                    transpose_x(3 * l + 3, range(TT))

        @block.scalar
        def _(act):
            def drain(name, dst, src, func=ACT.Copy, **how):
                wait_filled(act, *name)
                act.activation(dst, src, func, **how).then_inc(*is_drained(*name))

            def high(dst, src, func=ACT.Copy, **how):
                act.activation(dst, src, func, **how).then_inc(hi_set, 1)

            def high_xt(site, ts=range(TT)):
                for t in ts:
                    for g in range(2):
                        wait_filled(act, "xt", site, t, g)
                        high(x_hi[:, 4 * g:4 * g + 4, t * P:(t + 1) * P],
                             bank("xt", site, t, g).rearrange("p (q s) -> p q s", q=4))

            def copy_xt(site, ts):
                for t in ts:
                    for g in range(2):
                        name = ("xt", site, t, g)
                        drain(name, xt[:, 4 * g:4 * g + 4, t * P:(t + 1) * P],
                              bank(*name).rearrange("p (q s) -> p q s", q=4))

            def split_weights(what, l, c):
                number = split_number(what, l, c)
                slot, uses, _ = tile_slots[what, l, c]
                wait_pair_free(act, number)
                for n in range(SPLIT_HALVES):
                    if number == 0 and n == 0:
                        act.wait_ge(half_landed, 16)
                    else:
                        act.wait_ge(landed[slot], 16 * uses)
                    ks = slice(n * split_chunks, (n + 1) * split_chunks)
                    act.activation(w_hi[number % 2][:, ks, :], tile_view(slot, KD)[:, ks, :], ACT.Copy).then_inc(w_hi_set, 1)

            def keys(l, c):
                for j in range(2):
                    n = 4 * c + 2 * j
                    drain(("k", l, c, j), kt[:, n:n + 2, :], bank("k", l, c, j).rearrange("p (q m) -> p q m", q=2))

            def values(l, c):
                for m in range(MT):
                    drain(("v", l, c, m), va[:, m, c * HALF:(c + 1) * HALF], bank("v", l, c, m))

            def even_mixer():
                high_xt(0, [0])
                split_weights("gate_v", 0, 0)
                high_xt(0, (1, 2))
                for t in range(TT):
                    if t == 1:
                        high_xt(0, (3,))
                        split_weights("pool_a", 0, 0)
                    drain(("gate_v", t), vn[:, t, :], bank("gate_v", t), ACT.Gelu_apprx_tanh)
                split_weights("gate_u", 0, 0)
                for m in range(4):
                    drain(("pool_a", m), at[:, m, PAD:PAD + S], bank("pool_a", m))
                split_weights("mix", 0, 0)
                for m in range(4):
                    drain(("gate_u", m), ut[:, m, :], bank("gate_u", m), ACT.Gelu_apprx_tanh)
                drain(("wst",), wst[:, :, :], bank("wst").rearrange("p (h i) -> p h i", h=SG_HEADS))
                act.wait_ge(rows_landed, 16 * 5)
                for g in range(4):
                    wait_filled(act, "pool_y", g)
                    high(x_hi[:, g, :], bank("pool_y", g), scale=pscale[:, g:g + 1])
                for h in range(SG_HEADS):
                    act.wait_ge(gated, h + 1)
                    high(x_hi[:, 4 + h, :], gate_rows[:, h, :])
                split_weights("mix", 0, 1)
                for m in range(MT):
                    for g in range(2):
                        drain(("memt", m, g), memt[:, 4 * g:4 * g + 4, m * P:(m + 1) * P],
                              bank("memt", m, g).rearrange("p (q s) -> p q s", q=4))
                for m in range(MT):
                    for g in range(2):
                        wait_drained(act, "memt", m, g)
                act.wait_ge(gated, SG_HEADS)
                high(mem_hi[:, :, :], memt[:, :, :])

            def odd_mixer():
                split_weights("z", 1, 0)
                for c in range(2):
                    for m in range(4):
                        if c:
                            wait_drained(act, "z", 0, m)
                        drain(("cg", c, m), cgt[:, m, :], bank("cg", c, m))
                    split_weights("bg", 1, c)
                    split_weights(*(("mix", 1, 0) if c else ("cg", 1, 1)))
                    if not c:
                        split_weights("z", 1, 1)
                for m in range(4):
                    wait_drained(act, "bg", 1, m)
                for t in range(TT):
                    high(x_hi[:, :, t * P:(t + 1) * P], mixt[:, :, t * P:(t + 1) * P])
                split_weights("mix", 1, 1)
                split_weights("q", 1, 0)

            def attention(l):
                split_weights("q", l, 1)
                for m in range(4):
                    drain(("q", l, 0, m), qt[:, m, :], bank("q", l, 0, m))
                split_weights("wo", l, 0)
                for m in range(4):
                    drain(("q", l, 1, m), qt[:, 4 + m, :], bank("q", l, 1, m))

                def exps(j):
                    act.wait_ge(smax_ready, 8 * l + j + 1)
                    for h in range(2):
                        e = act.activation(work[:, j % 2, h * MEM:(h + 1) * MEM], bank("s", l, j)[:, h * MEM:(h + 1) * MEM],
                                           ACT.Exp, bias=nsmax[:, j % 2, h:h + 1], scale=SCALE,
                                           accum_out=ssum[:, j % 2, h:h + 1])
                    e.then_inc(*is_drained("s", l, j))

                exps(0)
                exps(1)
                def high_outputs(ns):
                    for n in ns:
                        wait_filled(act, "o", l, n)
                        high(o_hi[:, n, :], bank("o", l, n))

                for j in range(8):
                    t, hp = j % TT, j // TT
                    high_outputs(O_BEFORE.get(j, ()))
                    drain(("pt", l, j), pt[:, 2 * hp:2 * hp + 2, :, t * P:(t + 1) * P],
                          bank("pt", l, j).rearrange("p (h m s) -> p h m s", h=2, m=MT))
                    if j + 2 < 8:
                        exps(j + 2)
                high_outputs(range(4, 8))
                split_weights("wo", l, 1)

            def pair(sig, u, i):
                p = 2 * i + u
                for j in (XG0, XG1):
                    sig.wait_filled(act, j, p)
                    g = 4 * (j - XG0)
                    act.activation(xgt[:, g:g + 4, :], ps[:, sig.bank(j), :].rearrange("p (q s) -> p q s", q=4),
                                   ACT.Copy).then_inc(sig.drained[sig.bank(j)], 1)
                for b, j in enumerate((HA, HB)):
                    sig.wait_filled(act, j, p)
                    act.activation(silu_sb[b], ps[0:SLOTS, sig.bank(j), :], ACT.Silu).then_inc(sig.silu, 1)
                for b, j in enumerate((TA, TB)):
                    sig.wait_filled(act, j, p)
                    act.activation(hidt[b], ps[:, sig.bank(j), 0:4 * SLOTS].rearrange("p (q s) -> p q s", q=4),
                                   ACT.Copy).then_inc(sig.drained[sig.bank(j)], 1)

            def experts(l):
                with act.Fori(0, main[l].rounds) as i:
                    for u in range(2):
                        pair(main[l], u, i)
                act.wait_ge(more_known, l + 1)
                count = act.value_load(more[0:1, 0:1], min_val=0, max_val=MORE_BLOCKS - 1)
                with act.If(count > 0):
                    with act.Fori(0, rest[l].rounds) as i:
                        for u in range(2):
                            pair(rest[l], u, i)

            for l in range(DEPTH):
                if l == 0:
                    even_mixer()
                    split_weights("k", 0, 0)
                    split_weights("k", 0, 1)
                    keys(0, 0)
                    split_weights("v", 0, 0)
                    keys(0, 1)
                    split_weights("v", 0, 1)
                    values(0, 0)
                    split_weights("q", 0, 0)
                    values(0, 1)
                else:
                    high_xt(3)
                    odd_mixer()
                high_xt(3 * l + 1)
                attention(l)
                copy_xt(3 * l + 2, range(3))
                if l == 0:
                    keys(1, 0)
                copy_xt(3 * l + 2, [3])
                if l == 0:
                    keys(1, 1)
                act.wait_ge(gate_in_ready, l + 1)
                act.activation(exp_g[:, :, :], exp_g[:, :, :], ACT.Exp).then_inc(gate_exp_ready, 1)
                act.activation(dexp, dexp, ACT.Exp).then_inc(gate_exp_ready, 1)
                if l == 0:
                    values(1, 0)
                    values(1, 1)
                experts(l)
                if l + 1 < DEPTH:
                    split_weights("cg", 1, 0)

        @block.vector
        def _(dve):
            steps = [0]
            norms = [0]
            centred = [0]

            def link(ins):
                steps[0] += 1
                ins.then_inc(dve_step, 1)
                dve.wait_ge(dve_step, steps[0])

            def measure(parts):
                turn = norms[0] % 2
                for n, part in enumerate(parts):
                    st = dve.bn_stats(stats[:, 6 * n:6 * n + 6], part)
                link(st)
                link(dve.bn_aggr(mean_var[turn][:, :], stats[:, 0:6 * len(parts)]))
                dve.tensor_scalar(var_eps[turn][:, :], mean_var[turn][:, 1:2], LN_EPS, None, ALU.add).then_inc(var_ready, 1)
                norms[0] += 1
                return norms[0]

            def normalize(row, norm):
                turn = (norm - 1) % 2
                dve.wait_ge(rstd_ready, norm)
                link(dve.tensor_scalar(row, row, mean_var[turn][:, 0:1], rstd[turn][:, 0:1], ALU.subtract, ALU.mult))

            highs = [0]

            def low(hi, lo, src):
                highs[0] += 1
                dve.wait_ge(hi_set, highs[0])
                return dve.tensor_tensor(lo, src, hi.bitcast(F32), ALU.subtract)

            def low_xt(site, t):
                for g in range(2):
                    cols = (slice(None), slice(4 * g, 4 * g + 4), slice(t * P, (t + 1) * P))
                    low(x_hi[cols], x_lo[cols], bank("xt", site, t, g).rearrange("p (q s) -> p q s", q=4))\
                        .then_inc(*is_drained("xt", site, t, g))

            def split_weights(what, l, c):
                number = split_number(what, l, c)
                slot, uses, _ = tile_slots[what, l, c]
                wait_pair_free(dve, number)
                for n in range(SPLIT_HALVES):
                    ks = slice(n * split_chunks, (n + 1) * split_chunks)
                    dve.wait_ge(w_hi_set, SPLIT_HALVES * number + n + 1)
                    dve.tensor_tensor(w_lo[number % 2][:, ks, :], tile_view(slot, KD)[:, ks, :],
                                      w_hi[number % 2][:, ks, :].bitcast(F32), ALU.subtract).then_inc(w_lo_set, 1)

            def layer_norm(site, residual, ahead=False, between=lambda t: None):
                read = [None] * TT

                def begin(t):
                    pieces, read[t] = residual(t)
                    return pieces, measure(pieces)

                def end(t, begun):
                    pieces, norm = begun
                    turn = (norm - 1) % 2
                    if t == 0:
                        dve.wait_ge(gb_landed, 32 * (site + 1))
                    width = D // len(pieces)
                    for n, piece in enumerate(pieces):
                        cols = slice(n * width, (n + 1) * width)
                        dve.scalar_tensor_tensor(out=xs[:, t, cols], in0=piece, scalar=mean_var[turn][:, 0:1],
                                                 in1=gb[:, 0, cols], op0=ALU.subtract, op1=ALU.mult)\
                            .then_inc(*read[t][n])
                    for signal, value in read[t][len(pieces):]:
                        dve.wait_ge(signal, value)
                    dve.wait_ge(rstd_ready, norm)
                    dve.scalar_tensor_tensor(out=xs[:, t, :], in0=xs[:, t, :], scalar=rstd[turn][:, 0:1], in1=gb[:, 1, :],
                                             op0=ALU.mult, op1=ALU.add).then_inc(x_ready, 1)

                begun = begin(0)
                for t in range(1, TT):
                    if ahead:
                        following = begin(t)
                        end(t - 1, begun)
                        begun = following
                    else:
                        end(t - 1, begun)
                        between(t)
                        begun = begin(t)
                end(TT - 1, begun)
                dve.wait_ge(x_ready, TT * (site + 1))

            def from_banks(what, l):
                def residual(t):
                    row = work[:, t % 2, :]
                    for c in range(2):
                        wait_filled(dve, what, l, t, c)
                        cols = slice(c * HALF, (c + 1) * HALF)
                        dve.scalar_tensor_tensor(out=row[:, cols], in0=xs[:, t, cols], scalar=ALPHA,
                                                 in1=bank(what, l, t, c), op0=ALU.mult, op1=ALU.add)\
                           .then_inc(*is_drained(what, l, t, c))
                    for c in range(2):
                        wait_drained(dve, what, l, t, c)
                    centred[0] += 2
                    return [row[:, 0:HALF], row[:, HALF:D]], [(row_centred, 1), (row_centred, 1), (row_centred, centred[0])]
                return residual

            def from_experts(l):
                def residual(t):
                    for c in range(2):
                        wait_filled(dve, "sum", l, t, c)
                    read = [is_drained("sum", l, t, c) for c in range(2)]
                    for c in range(2):
                        n = jobs["sum", l, t, c]
                        read.append((drained[n % BANKS], n // BANKS + 1))
                    return [bank("sum", l, t, c) for c in range(2)], read
                return residual

            def even_mixer():
                link(dve.memset(at[:, :, 0:PAD], 0.0))
                for n in range(PAD):
                    c = dve.memset(inv_count[:, n:n + 1], 1.0 / (n + 1))
                link(c)
                dve.wait_ge(rows_landed, 16 * 5)
                for t in range(TT):
                    wait_drained(dve, "gate_v", t)
                    v = vn[:, t, :]
                    normalize(v, measure([v]))
                    link(dve.tensor_tensor(v, v, lnvg, ALU.mult))
                    dve.tensor_tensor(v, v, lnvb, ALU.add).then_inc(vn_ready, 1)
                split_weights("gate_u", 0, 0)
                for g, w in enumerate(WINDOWS):
                    wait_drained(dve, "pool_a", g)
                    src, span, turn = at[:, g, :], 1, 0
                    while span < w:
                        dst = work[:, turn, 0:PAD + S]
                        link(dve.tensor_tensor(dst[:, 2 * span - 1:], src[:, 2 * span - 1:], src[:, span - 1:PAD + S - span], ALU.add))
                        src, span, turn = dst, 2 * span, 1 - turn
                    a = at[:, g, PAD:]
                    link(dve.scalar_tensor_tensor(out=dt_[:, g, :], in0=src[:, PAD:], scalar=1.0 / w, in1=a,
                                                  op0=ALU.mult, op1=ALU.subtract))
                    head = src[:, PAD:PAD + w - 1]
                    link(dve.tensor_tensor(head, head, inv_count[:, 0:w - 1], ALU.mult))
                    dve.tensor_tensor(dt_[:, g, 0:w - 1], head, a[:, 0:w - 1], ALU.subtract).then_inc(pooled, 1)
                    dve.wait_ge(pooled, g + 1)
                split_weights("mix", 0, 0)
                for h in range(SG_HEADS):
                    wait_filled(dve, "spatial", h)
                    gate = gate_rows[:, h, :]
                    dve.tensor_tensor(gate.rearrange("p (t i) -> p t i", t=TT),
                                      bank("spatial", h).rearrange("p (t i) -> p t i", t=TT),
                                      bsp[:, h:h + 1, :].broadcast_to([P, TT, P]), ALU.add)\
                       .then_inc(*is_drained("spatial", h))
                    wait_drained(dve, "spatial", h)
                    wait_drained(dve, "gate_u", h)
                    dve.tensor_tensor(gate, gate, ut[:, h, :], ALU.mult).then_inc(gated, 1)
                for g in range(4):
                    highs[0] += 1
                    dve.wait_ge(hi_set, highs[0])
                    dve.scalar_tensor_tensor(out=x_lo[:, g, :], in0=bank("pool_y", g), scalar=pscale[:, g:g + 1],
                                             in1=x_hi[:, g, :].bitcast(F32), op0=ALU.mult, op1=ALU.subtract)\
                        .then_inc(*is_drained("pool_y", g))
                for h in range(SG_HEADS):
                    low(x_hi[:, 4 + h, :], x_lo[:, 4 + h, :], gate_rows[:, h, :]).then_inc(mixt_ready, 1)
                split_weights("mix", 0, 1)
                low(mem_hi[:, :, :], mem_lo[:, :, :], memt[:, :, :]).then_inc(mem_lo_set, 1)

            def odd_mixer():
                split_weights("z", 1, 0)
                link(dve.memset(zct[:, :, 0:2], 0.0))
                for c in range(2):
                    split_weights("bg", 1, c)
                    for m in range(4):
                        wait_filled(dve, "z", c, m)
                        wait_drained(dve, "cg", c, m)
                        dve.tensor_tensor(zct[:, m, 2:], bank("z", c, m), cgt[:, m, :], ALU.mult)\
                           .then_inc(*is_drained("z", c, m))
                    split_weights(*(("mix", 1, 0) if c else ("cg", 1, 1)))
                    for m in range(4):
                        n = 4 * c + m
                        wait_drained(dve, "z", c, m)
                        conv = mixt[:, n, :]
                        link(dve.tensor_scalar(conv, zct[:, m, 0:S], convw[:, n, 0:1], convb[:, n:n + 1], ALU.mult, ALU.add))
                        for tap in (1, 2):
                            link(dve.scalar_tensor_tensor(out=conv, in0=zct[:, m, tap:tap + S], scalar=convw[:, n, tap:tap + 1],
                                                          in1=conv, op0=ALU.mult, op1=ALU.add))
                        wait_filled(dve, "bg", c, m)
                        dve.tensor_tensor(conv, bank("bg", c, m), conv, ALU.mult).then_inc(*is_drained("bg", c, m))
                        wait_drained(dve, "bg", c, m)
                    if not c:
                        split_weights("z", 1, 1)
                for t in range(TT):
                    cols = (slice(None), slice(None), slice(t * P, (t + 1) * P))
                    low(x_hi[cols], x_lo[cols], mixt[cols]).then_inc(mixt_ready, 1)
                split_weights("mix", 1, 1)

            def attention(l):
                def find_max(j):
                    wait_filled(dve, "s", l, j)
                    link(dve.tensor_reduce(smax[:, j % 2, :], bank("s", l, j).rearrange("p (h m) -> p h m", h=2), AX.X, ALU.max))
                    dve.tensor_scalar(nsmax[:, j % 2, :], smax[:, j % 2, :], -SCALE, None, ALU.mult).then_inc(smax_ready, 1)

                split_weights("q", l, 1)
                split_weights("wo", l, 0)
                find_max(0)
                find_max(1)
                for j in range(8):
                    wait_drained(dve, "s", l, j)
                    link(dve.reciprocal(srec[:, j % 2, :], ssum[:, j % 2, :]))
                    for h in range(2):
                        p = work[:, j % 2, h * MEM:(h + 1) * MEM]
                        s = dve.tensor_scalar(p, p, srec[:, j % 2, h:h + 1], None, ALU.mult)
                    s.then_inc(p_ready, 1)
                    if j + 2 < 8:
                        find_max(j + 2)
                for n in range(8):
                    low(o_hi[:, n, :], o_lo[:, n, :], bank("o", l, n)).then_inc(*is_drained("o", l, n))
                split_weights("wo", l, 1)

            def first_of(cands, values, top, iota, least, onehot):
                shape = list(values.shape)
                link(dve.tensor_tensor(cands, values, top.unsqueeze(2).broadcast_to(shape), ALU.is_equal))
                link(dve.scalar_tensor_tensor(out=cands, in0=cands, scalar=-100.0, in1=iota.unsqueeze(1).broadcast_to(shape),
                                              op0=ALU.mult, op1=ALU.add))
                link(dve.tensor_reduce(least, cands, AX.X, ALU.min))
                link(dve.tensor_tensor(onehot, cands, least.unsqueeze(2).broadcast_to(shape), ALU.is_equal))

            def take_logits(l, ts):
                for t in ts:
                    wait_filled(dve, "route", l, t)
                    dve.tensor_tensor(logits[:, t, :], bank("route", l, t)[:, 0:NROUTE], br[:, :], ALU.add)\
                       .then_inc(*is_drained("route", l, t))

            def router(l):
                link(dve.memset(chosen[:, TT * EXPERTS:], 0.0))
                take_logits(l, (2, 3))
                for t in range(TT):
                    wait_drained(dve, "route", l, t)
                lg = logits[:, :, 0:GROUPS]
                link(dve.tensor_reduce(gmax, lg, AX.X, ALU.max))
                first_of(cand_g, lg, gmax, iota_e[:, 0:GROUPS], gmin, oh_g)
                link(dve.tensor_scalar(oh_g, oh_g, -1.0, BIG, ALU.add, ALU.mult))
                link(dve.tensor_tensor(lm.rearrange("p t (g e) -> p t g e", g=GROUPS),
                                       logits[:, :, GROUPS:].rearrange("p t (g e) -> p t g e", g=GROUPS),
                                       oh_g.unsqueeze(3).broadcast_to([P, TT, GROUPS, PER_GROUP]), ALU.add))
                link(dve.tensor_reduce(v0, lm, AX.X, ALU.max))
                first_of(cand, lm, v0, iota_e[:, :], scr, oh[0])
                link(dve.scalar_tensor_tensor(out=lm, in0=oh[0], scalar=-3 * BIG, in1=lm, op0=ALU.mult, op1=ALU.add))
                link(dve.tensor_reduce(v1, lm, AX.X, ALU.max))
                first_of(cand, lm, v1, iota_e[:, :], scr, oh[1])
                dve.tensor_tensor(chosen[:, 0:TT * EXPERTS].rearrange("p (t e) -> p t e", t=TT), oh[0], oh[1], ALU.add)\
                   .then_inc(chosen_ready, 1)
                link(dve.tensor_tensor(exp_g, lg, gmax.unsqueeze(2).broadcast_to([P, TT, GROUPS]), ALU.subtract))
                dve.tensor_tensor(dexp, v1, v0, ALU.subtract).then_inc(gate_in_ready, 1)

                for n in range(2):
                    link(dve.memset(scan[n][:, 0:EXPERTS // 2], 0.0))
                dve.memset(xg[0], 0.0).then_inc(xg_cleared, 1)

                wait_filled(dve, "rank", l)
                dve.tensor_copy(rank_i, bank("rank", l)[:, 0:TT * EXPERTS].rearrange("p (t e) -> p t e", t=TT))
                dve.tensor_scalar(extra_i, bank("rank", l)[:, TT * EXPERTS:(TT + 1) * EXPERTS], float(SLOTS - 1), None, ALU.add)\
                   .then_inc(*is_drained("rank", l))
                wait_drained(dve, "rank", l)
                shift = SLOTS.bit_length() - 1
                link(dve.tensor_scalar(rank_hi, rank_i, shift, None, ALU.logical_shift_right))
                link(dve.tensor_scalar(rank_i, rank_i, SLOTS - 1, None, ALU.bitwise_and))
                link(dve.tensor_scalar(extra_i, extra_i, shift, None, ALU.logical_shift_right))
                head, span, turn = EXPERTS // 2, 1, 0
                link(dve.tensor_scalar(scan[0][:, head:], extra_i, -1.0, 0.0, ALU.add, ALU.max))
                while span < EXPERTS:
                    src, dst = scan[turn], scan[1 - turn]
                    link(dve.tensor_tensor(dst[:, head:], src[:, head:], src[:, head - span:head - span + EXPERTS], ALU.add))
                    span, turn = 2 * span, 1 - turn
                link(dve.tensor_tensor(base_n, below_n, first_more[:, :], ALU.add))
                rows = [P, TT, EXPERTS]
                link(dve.scalar_tensor_tensor(out=slot, in0=rank_hi, scalar=0.0, in1=base_n.unsqueeze(1).broadcast_to(rows),
                                              op0=ALU.is_gt, op1=ALU.mult))
                link(dve.tensor_tensor(slot, slot, rank_hi, ALU.add))
                link(dve.tensor_tensor(slot, slot, iota_e[:, :].unsqueeze(1).broadcast_to(rows), ALU.add))
                link(dve.scalar_tensor_tensor(out=slot, in0=rank_i, scalar=float(SLOTS), in1=slot, op0=ALU.mult, op1=ALU.add))
                for c in range(2):
                    link(dve.tensor_tensor(cand, oh[c], slot, ALU.mult))
                    link(dve.tensor_reduce(place_n[:, c * TT:(c + 1) * TT], cand, AX.X, ALU.add))
                link(dve.tensor_copy(place[:, :], place_n))
                link(dve.tensor_scalar(place_lo[:, :], place[:, :], SLOTS - 1, None, ALU.bitwise_and))
                link(dve.tensor_scalar(place[:, :], place[:, :], shift, None, ALU.logical_shift_right))
                half = [P, 2 * TT, SLOTS]
                for h in range(2):
                    dve.tensor_tensor(at_slot[:, :, h * SLOTS:(h + 1) * SLOTS], place[:, :].unsqueeze(2).broadcast_to(half),
                                      iota_s[:, :].unsqueeze(1).broadcast_to(half), ALU.is_equal)
                wide = [P, 2 * TT, BLOCKS]
                link(dve.tensor_tensor(at_block, place_lo[:, :].unsqueeze(2).broadcast_to(wide),
                                       iota_s[:, 0:BLOCKS].unsqueeze(1).broadcast_to(wide), ALU.is_equal))
                dve.tensor_tensor(at_block, at_block, number_a[:, :].unsqueeze(2).broadcast_to(wide), ALU.mult)\
                   .then_inc(place_ready, 1)

                dve.memset(xg[1], 0.0).then_inc(xg_cleared, 1)

                wait_filled(dve, "table", l)
                dve.tensor_scalar(raw[:, :], bank("table", l)[:, 0:BLOCKS], float(INVALID), None, ALU.add)\
                   .then_inc(*is_drained("table", l))
                wait_drained(dve, "table", l)
                dve.tensor_scalar(from_row[0:SLOTS, :], raw[0:SLOTS, 0:BLOCKS:2], 1, None, ALU.logical_shift_right)\
                   .then_inc(rows_known, 1)
                dve.tensor_scalar(from_row[SLOTS:P, :], raw[SLOTS:P, 1:BLOCKS:2], 1, None, ALU.logical_shift_right)\
                   .then_inc(rows_known, 1)
                dve.tensor_scalar(to_row[:, :], raw[:, :], 2.0, upper[:, 0:1], ALU.mult, ALU.add).then_inc(rows_known, 1)

                shape = [P, MORE_BLOCKS, EXPERTS]
                link(dve.tensor_tensor(more_x, upto_n.unsqueeze(1).broadcast_to(shape),
                                       iota_e[:, 0:MORE_BLOCKS].unsqueeze(2).broadcast_to(shape), ALU.is_le))
                link(dve.tensor_reduce(more_n, more_x, AX.X, ALU.add))
                link(dve.tensor_copy(more[:, 0:1], upto_n[:, EXPERTS - 1:EXPERTS]))
                dve.tensor_scalar(more[:, 1:], more_n, float(EXPERTS - 1), None, ALU.min).then_inc(more_known, 1)

                dve.wait_ge(gate_exp_ready, 2 * (l + 1))
                link(dve.tensor_reduce(gsum, exp_g, AX.X, ALU.add))
                link(dve.scalar_tensor_tensor(out=gsum, in0=dexp, scalar=1.0, in1=gsum, op0=ALU.add, op1=ALU.mult))
                link(dve.reciprocal(scr, gsum))
                link(dve.tensor_copy(gates[:, :, 0:1], scr.unsqueeze(2)))
                link(dve.tensor_tensor(gates[:, :, 1:2], scr.unsqueeze(2), dexp.unsqueeze(2), ALU.mult))
                for t in range(TT):
                    for c in range(2):
                        dve.tensor_scalar(diag[:, 2 * t + c, :], ident[:, :], gates[:, t, c:c + 1], None, ALU.mult)
                dve.tensor_scalar(diag[:, 2 * TT, :], ident[:, :], ALPHA, None, ALU.mult).then_inc(diag_set, 1)

            def pair(sig, u, i):
                p = 2 * i + u
                for b, j in enumerate((HA, HB)):
                    dve.wait_ge(sig.silu, sig.silu0 + 2 * p + b + 1)
                    dve.tensor_tensor(hid[b].rearrange("s (q p) -> s p q", q=4),
                                      silu_sb[b].rearrange("s (p q) -> s p q", q=4),
                                      ps[SLOTS:P, sig.bank(j), :].rearrange("s (p q) -> s p q", q=4), ALU.mult)\
                       .then_inc(sig.drained[sig.bank(j)], 1)
                for b, j in enumerate((YA, YB)):
                    dve.wait_ge(sig.index_ready[u][b], sig.index0[u] + i + 1)
                    sig.wait_filled(dve, j, p)
                    dve.tensor_copy(ysb[u][b], ps[:, sig.bank(j), :]).then_inc(sig.drained[sig.bank(j)], 1)

            def experts(l):
                with dve.Fori(0, main[l].rounds) as i:
                    for u in range(2):
                        pair(main[l], u, i)
                dve.wait_ge(more_known, l + 1)
                count = dve.value_load(more[0:1, 0:1], min_val=0, max_val=MORE_BLOCKS - 1)
                with dve.If(count > 0):
                    with dve.Fori(0, rest[l].rounds) as i:
                        for u in range(2):
                            pair(rest[l], u, i)

            low_xt(0, 0)
            split_weights("gate_v", 0, 0)
            for t in range(1, TT):
                low_xt(0, t)
            split_weights("pool_a", 0, 0)
            for l in range(DEPTH):
                dve.wait_ge(consts_set, 1)
                if l == 0:
                    even_mixer()
                    layer_norm(3 * l, from_banks("mix", l),
                               between=lambda t: split_weights("k", 0, 0) if t == 2 else None)
                    split_weights("k", 0, 1)
                    for c in range(2):
                        split_weights("v", 0, c)
                    split_weights("q", 0, 0)
                else:
                    odd_mixer()
                    layer_norm(3 * l, from_banks("mix", l),
                               between=lambda t: split_weights("q", 1, 0) if t == 2 else None)
                for t in range(TT):
                    low_xt(3 * l + 1, t)
                attention(l)
                layer_norm(3 * l + 1, from_banks("wo", l),
                           between=lambda t: take_logits(l, ROUTE_FIRST) if t == 3 else None)
                router(l)
                experts(l)
                if l + 1 < DEPTH:
                    split_weights("cg", 1, 0)
                    layer_norm(3 * l + 2, from_experts(l), ahead=True)
                    for t in range(TT):
                        low_xt(3 * l + 3, t)
                else:
                    layer_norm(3 * l + 2, from_experts(l), ahead=True)

        @block.gpsimd
        def _(pool):
            sets = [0]
            norms = [0]

            def link(ins):
                sets[0] += 1
                ins.then_inc(pool_set, 1)
                pool.wait_ge(pool_set, sets[0])

            def powers(n):
                for _ in range(n):
                    turn = norms[0] % 2
                    norms[0] += 1
                    pool.wait_ge(var_ready, norms[0])
                    pool.tensor_tensor(rstd[turn][:, :], var_eps[turn][:, :], minus_half[:, :], ALU.pow).then_inc(rstd_ready, 1)

            def load_gb(site):
                if site:
                    pool.wait_ge(x_ready, TT * site)
                else:
                    for m in range(MT):
                        for g in range(2):
                            wait_filled(pool, "memt", m, g)
                l, n = site // 3, site % 3
                for c, v in enumerate((ln_g, ln_b)):
                    pool.dma_start(gb[:, c, :], v[l, n:n + 1, :].partition_broadcast(P)).then_inc(gb_landed, 16)

            def load_router(l):
                for g in range(GROUPS):
                    at_ = GROUPS + g * PER_GROUP
                    pool.dma_start(wr[:, :, at_:at_ + PER_GROUP], wr_expert[l, g].rearrange("(k p) e -> p k e", p=P))\
                        .then_inc(router_landed, 16)
                pool.dma_start(wr[:, :, 0:GROUPS], wr_group[l].rearrange("(k p) g -> p k g", p=P)).then_inc(router_landed, 16)

            def load_biases(l):
                pool.dma_start(br[:, 0:GROUPS], br_group[l:l + 1, :].partition_broadcast(P)).then_inc(rows_landed, 16)
                pool.dma_start(br[:, GROUPS:], br_expert[l:l + 1].rearrange("o g e -> o (g e)").partition_broadcast(P))\
                    .then_inc(rows_landed, 16)

            def dispatch(l):
                for t in range(TT):
                    pool.dma_start(x_dram[l][t * P:(t + 1) * P, :], xs[:, t, :]).then_inc(x_stored, 16)
                pool.wait_ge(rows_known, 3 * (l + 1))
                pool.wait_ge(x_stored, 16 * TT * (l + 1))
                pool.wait_ge(xg_cleared, 2 * (l + 1))

            last_row = pool.to_reg(S - 1)
            last_half = pool.to_reg(4 * S - 1)

            def gather(l, sig, u, p, step):
                pool.tensor_copy(gather_index[u][:, :], from_row[:, bass.ds(p, 1)]).then_inc(sig.pool_step, 1)
                pool.wait_ge(sig.pool_step, step)
                pool.sem_inc(index_seen, 1)
                pool.indirect_dma_start(xg[u], None, x_dram[l], bass.IndirectOffsetOnAxis(ap=gather_index[u][:, 0:1], axis=0),
                                        bounds_check=last_row, oob_is_err=False).then_inc(sig.gathered[u], 16)

            def set_index(sig, u, b, p):
                pool.tensor_copy(store_index[u][b][:, :], to_row[:, bass.ds(2 * p + b, 1)])\
                    .then_inc(sig.index_ready[u][b], 1)

            def step(l, sig, u, i):
                p = 2 * i + u
                sig.wait_filled(pool, XG1, p)
                pool.wait_ge(sig.gathered[u], 16 * (sig.gathered0 + 1 + i))
                gather(l, sig, u, p + (sig.pair0 + 2), p + (sig.step0 + 3))
                for b in range(2):
                    if u or sig.stored0 or not isinstance(i, int):
                        pool.wait_ge(sig.stored[1 - u][b], 16 * (sig.stored0 + i + u))
                    set_index(sig, 1 - u, b, p + (sig.pair0 + 1))
                for b, j in enumerate((YA, YB)):
                    sig.wait_drained(pool, j, p)
                    pool.wait_ge(sig.index_ready[u][b], sig.index0[u] + 1 + i)
                    pool.sem_inc(index_seen, 1)
                    pool.indirect_dma_start(y_dram[l], bass.IndirectOffsetOnAxis(ap=store_index[u][b][:, 0:1], axis=0),
                                            ysb[u][b], None, bounds_check=last_half, oob_is_err=False)\
                        .then_inc(sig.stored[u][b], 16)

            def pairs(l, sig):
                for u in range(2):
                    gather(l, sig, u, sig.pair0 + u, sig.step0 + u + 1)
                for b in range(2):
                    set_index(sig, 0, b, sig.pair0)
                for u in range(2):
                    step(l, sig, u, 0)
                with pool.Fori(1, sig.rounds) as i:
                    for u in range(2):
                        step(l, sig, u, i)
                for u in range(2):
                    pool.wait_ge(sig.gathered[u], 16 * (sig.gathered0 + 1 + sig.rounds))
                    for b in range(2):
                        pool.wait_ge(sig.stored[u][b], 16 * (sig.stored0 + sig.rounds))
                        pool.wait_ge(sig.index_ready[u][b], sig.index0[u] + sig.rounds + 1 - u)

            def experts(l):
                pairs(l, main[l])
                count = pool.value_load(more[0:1, 0:1], min_val=0, max_val=MORE_BLOCKS - 1)
                with pool.If(count > 0):
                    pairs(l, rest[l])

            link(pool.memset(ident[:, :], 0.0))
            pool.affine_select(out=ident[:, :], in_=ident[:, :], compare_op=ALU.not_equal, fill=1.0, base=0,
                               pattern=[[-1, P]], channel_multiplier=1).then_inc(ident_set, 1)
            link(pool.memset(ones[:, :], 1.0))
            pool.affine_select(out=before[:, :], in_=ones[:, :], compare_op=ALU.is_gt, fill=0.0, base=0,
                               pattern=[[1, P]], channel_multiplier=-1).then_inc(ident_set, 1)
            link(pool.memset(minus_half[:, :], -0.5))
            pool.dma_start(wst, w_spatial[0].rearrange("h i j -> i h j")).then_inc(even_landed, 16)
            pool.dma_start(wpool, w_pool[0].rearrange("g c d -> c g d")).then_inc(even_landed, 16)
            pool.dma_start(bsp, b_spatial[0:1].partition_broadcast(P)).then_inc(even_landed, 16)
            pool.dma_start(lnvg, ln_v_g[0:1, :].partition_broadcast(P)).then_inc(rows_landed, 16)
            pool.dma_start(lnvb, ln_v_b[0:1, :].partition_broadcast(P)).then_inc(rows_landed, 16)
            pool.dma_start(pscale[:, :], pool_scale[0].rearrange("(g p) -> p g", p=P),
                           allow_slow_non_contiguous=True).then_inc(rows_landed, 16)
            load_biases(0)
            pool.wait_ge(even_landed, 48)
            pool.affine_select(out=wst, in_=wst, compare_op=ALU.is_ge, fill=0.0, base=0,
                               pattern=[[0, SG_HEADS], [-1, P]], channel_multiplier=1).then_inc(tril_set, 1)
            pool.dma_start(convw[:, :, :], conv_w[0].rearrange("(k p) w -> p k w", p=P)).then_inc(even_landed, 16)
            pool.dma_start(convb[:, :], conv_b[0].rearrange("(k p) -> p k", p=P), allow_slow_non_contiguous=True).then_inc(even_landed, 16)
            pool.iota(iota_e[:, :], [[1, EXPERTS]], base=0, channel_multiplier=0, allow_small_or_imprecise_dtypes=True)
            pool.iota(first_more[:, :], [[-1, EXPERTS]], base=EXPERTS - 1, channel_multiplier=0,
                      allow_small_or_imprecise_dtypes=True)
            pool.iota(number_a[:, :].rearrange("p (c t) -> p c t", c=2), [[1, 2], [2 * P, TT]], base=-INVALID,
                      channel_multiplier=2, allow_small_or_imprecise_dtypes=True)
            pool.iota(iota_s[:, :], [[1, SLOTS]], base=0, channel_multiplier=0, allow_small_or_imprecise_dtypes=True)
            link(pool.memset(upper[0:SLOTS, :], 0.0))
            link(pool.memset(upper[SLOTS:P, :], 1.0))
            load_router(0)
            pool.wait_ge(even_landed, 80)
            pool.engine_nop().then_inc(consts_set, 1)
            powers(TT)
            load_gb(0)
            for l in range(DEPTH):
                powers(TT)
                load_gb(3 * l + 1)
                powers(TT)
                load_gb(3 * l + 2)
                dispatch(l)
                if l + 1 < DEPTH:
                    load_router(l + 1)
                    load_biases(l + 1)
                experts(l)
                powers(TT)
                if l + 1 < DEPTH:
                    load_gb(3 * l + 3)


_INS = ["x", "mem", "w_in_even", "w_pool", "pool_scale", "ln_v_g", "ln_v_b", "w_spatial", "b_spatial",
        "w_out_even", "w_in_odd", "conv_w", "conv_b", "w_out_odd", "wq_x", "wk_x", "wv_x", "wo_x",
        "ln_g", "ln_b", "wr_group", "br_group", "wr_expert", "br_expert", "w1", "w3", "w2"]


def kernel(**inputs):
    import numpy as _np
    import concourse.bacc as _bacc
    from concourse import mybir as _mybir
    from concourse.bass_utils import run_bass_kernel_spmd as _run

    nc = _bacc.Bacc("TRN2", target_bir_lowering=False, num_devices=1)
    arrays, args = {}, []
    for name in _INS:
        a = _np.ascontiguousarray(inputs[name])
        arrays[f"in_{name}_dram"] = a
        args.append(nc.dram_tensor(f"in_{name}_dram", a.shape, _mybir.dt.from_np(a.dtype), kind="ExternalInput").ap())
    args.append(nc.dram_tensor("out_0_dram", (1, S, D), F32, kind="ExternalOutput").ap())
    trunk(nc, *args)
    r = _run(nc, [arrays], core_ids=[0])
    return r.results[0]["out_0_dram"]
```
